# Optimizing a Trainium2 kernel written in Bass

```python
import jax, jax.numpy as jnp
from jax import lax
import numpy as np

D_MODEL = 2048
BATCH = 1
SEQ = 512
DEPTH = 1

D_MIX = D_MODEL
HEAD_DIM = 64
RWKV_WIDTH = D_MIX // 2
FOX_WIDTH = D_MIX - RWKV_WIDTH
RWKV_HEADS = RWKV_WIDTH // HEAD_DIM
FOX_HEADS = FOX_WIDTH // HEAD_DIM
DECAY_LORA = max(32, int(round(1.8 * D_MODEL ** 0.5 / 32)) * 32)
ICLR_LORA = max(32, int(round(1.8 * D_MODEL ** 0.5 / 32)) * 32)
GATE_LORA = max(32, int(round(0.6 * D_MODEL ** 0.8 / 32)) * 32)
RWKV_COLS = 3 * RWKV_WIDTH + DECAY_LORA + ICLR_LORA + GATE_LORA
FOX_COLS = 3 * FOX_WIDTH + FOX_HEADS
N_IN = RWKV_COLS + FOX_COLS
D_FF = -(-(8 * D_MODEL) // (3 * 256)) * 256
PLE_DIM = 256
BLOCK_Q = 128
RMS_EPS = 1e-6
GN_EPS = 64e-5

kernel_name = "rwkv7_fox_hybrid_layer"

def rmsnorm(x, g, eps=RMS_EPS):
    xf = x.astype(jnp.float32)
    y = xf * lax.rsqrt(jnp.mean(xf * xf, axis=-1, keepdims=True) + eps)
    return (y * g.astype(jnp.float32)).astype(x.dtype)

def token_shift(u):
    return jnp.pad(u, ((0, 0), (1, 0), (0, 0)))[:, :-1]

def rwkv7_scan(r, w, k, v, kk, a):
    b, s, h, n = r.shape
    seq_first = lambda t: jnp.swapaxes(t, 0, 1)

    def step(state, inp):
        r_t, w_t, k_t, v_t, kk_t, a_t = inp
        sa = jnp.einsum('bhvk,bhk->bhv', state, -kk_t)
        state = (state * w_t[:, :, None, :]
                 + sa[..., None] * (kk_t * a_t)[:, :, None, :]
                 + v_t[..., None] * k_t[:, :, None, :])
        y_t = jnp.einsum('bhvk,bhk->bhv', state, r_t)
        return state, y_t

    state0 = jnp.zeros((b, h, n, n), jnp.float32)
    _, y = lax.scan(step, state0, tuple(seq_first(t) for t in (r, w, k, v, kk, a)))
    return seq_first(y)

def rwkv7_mix(u, mu, w0, w2, a0, a2, g2, k_k, k_a, r_k, lnx_g, lnx_b):
    b, s, _ = u.shape
    u = (u + (token_shift(u) - u) * mu).astype(jnp.float32)
    r, k, v, xw, xa, xg = jnp.split(
        u, np.cumsum([RWKV_WIDTH, RWKV_WIDTH, RWKV_WIDTH, DECAY_LORA, ICLR_LORA]).tolist(), axis=-1)
    w_log = -jax.nn.softplus(-(w0 + jnp.tanh(xw) @ w2)) - 0.5
    decay = jnp.exp(-jnp.exp(w_log))
    a = jax.nn.sigmoid(a0 + xa @ a2)
    g = jax.nn.sigmoid(xg) @ g2
    heads = lambda t: t.reshape(b, s, RWKV_HEADS, HEAD_DIM)
    kk = heads(k * k_k)
    kk = kk / jnp.maximum(jnp.linalg.norm(kk, axis=-1, keepdims=True), 1e-12)
    k = k * (1.0 + (a - 1.0) * k_a)
    rh, kh, vh = heads(r), heads(k), heads(v)
    y = rwkv7_scan(rh, heads(decay), kh, vh, kk, heads(a))
    mean = jnp.mean(y, axis=-1, keepdims=True)
    var = jnp.mean(jnp.square(y - mean), axis=-1, keepdims=True)
    y = ((y - mean) * lax.rsqrt(var + GN_EPS)).reshape(b, s, RWKV_WIDTH) * lnx_g + lnx_b
    bonus = jnp.sum(rh * kh * r_k, axis=-1, keepdims=True) * vh
    y = (y + bonus.reshape(b, s, RWKV_WIDTH)) * g
    return y

def fox_mix(u, q_norm_g, k_norm_g, fgate_b):
    b, s, _ = u.shape
    q, k, v, f_raw = jnp.split(u, [FOX_WIDTH, 2 * FOX_WIDTH, 3 * FOX_WIDTH], axis=-1)
    heads = lambda t: t.reshape(b, s, FOX_HEADS, HEAD_DIM).astype(jnp.float32)
    q = rmsnorm(heads(q), q_norm_g)
    k = rmsnorm(heads(k), k_norm_g)
    v = heads(v)
    log_f = jax.nn.log_sigmoid(f_raw.astype(jnp.float32) + fgate_b)
    c = jnp.cumsum(log_f, axis=1).transpose(0, 2, 1)
    scale = HEAD_DIM ** -0.5
    outs = []
    for blk in range(s // BLOCK_Q):
        s0, s1 = blk * BLOCK_Q, (blk + 1) * BLOCK_Q
        scores = jnp.einsum('bqhd,bkhd->bhqk', q[:, s0:s1], k[:, :s1]) * scale
        bias = c[:, :, s0:s1, None] - c[:, :, None, :s1]
        causal = jnp.arange(s1)[None, :] <= (s0 + jnp.arange(BLOCK_Q))[:, None]
        scores = jnp.where(causal, scores + bias, -jnp.inf)
        probs = jax.nn.softmax(scores, axis=-1)
        outs.append(jnp.einsum('bhqk,bkhd->bqhd', probs, v[:, :s1]))
    return jnp.concatenate(outs, axis=1).reshape(b, s, FOX_WIDTH)

def setup_inputs(seed: int = 0) -> dict:
    key = jax.random.key(seed)
    ks = jax.random.split(key, 32)
    nrm = lambda k, shape, sc: jax.random.normal(k, shape, jnp.float32) * sc
    uni = lambda k, shape, lo, hi: jax.random.uniform(k, shape, jnp.float32, lo, hi)
    L = DEPTH
    return {
        "x": nrm(ks[0], (BATCH, SEQ, D_MODEL), 1.0),
        "p": nrm(ks[1], (DEPTH, BATCH, SEQ, PLE_DIM), 1.0),
        "attn_norm_g": 1.0 + nrm(ks[2], (L, D_MODEL), 0.02),
        "w_in": nrm(ks[3], (L, D_MODEL, N_IN), D_MODEL ** -0.5),
        "shift_mu": uni(ks[4], (L, RWKV_COLS), 0.0, 1.0),
        "w0": uni(ks[5], (L, RWKV_WIDTH), -6.0, 1.0),
        "w2": nrm(ks[6], (L, DECAY_LORA, RWKV_WIDTH), 0.5 * DECAY_LORA ** -0.5),
        "a0": nrm(ks[7], (L, RWKV_WIDTH), 0.1),
        "a2": nrm(ks[8], (L, ICLR_LORA, RWKV_WIDTH), 0.5 * ICLR_LORA ** -0.5),
        "g2": nrm(ks[9], (L, GATE_LORA, RWKV_WIDTH), GATE_LORA ** -0.5),
        "k_k": 0.85 + nrm(ks[10], (L, RWKV_WIDTH), 0.05),
        "k_a": 1.0 + nrm(ks[11], (L, RWKV_WIDTH), 0.05),
        "r_k": nrm(ks[12], (L, RWKV_HEADS, HEAD_DIM), 0.1),
        "lnx_g": 1.0 + nrm(ks[13], (L, RWKV_WIDTH), 0.02),
        "lnx_b": nrm(ks[14], (L, RWKV_WIDTH), 0.02),
        "q_norm_g": 1.0 + nrm(ks[15], (L, HEAD_DIM), 0.02),
        "k_norm_g": 1.0 + nrm(ks[16], (L, HEAD_DIM), 0.02),
        "fgate_b": uni(ks[17], (L, FOX_HEADS), 1.0, 6.0),
        "w_out": nrm(ks[18], (L, D_MIX, D_MODEL), D_MIX ** -0.5),
        "ffn_norm_g": 1.0 + nrm(ks[19], (L, D_MODEL), 0.02),
        "w_gate": nrm(ks[20], (L, D_MODEL, D_FF), D_MODEL ** -0.5),
        "w_up": nrm(ks[21], (L, D_MODEL, D_FF), D_MODEL ** -0.5),
        "w_down": nrm(ks[22], (L, D_FF, D_MODEL), D_FF ** -0.5),
        "ple_proj": nrm(ks[23], (L, PLE_DIM, D_MODEL), PLE_DIM ** -0.5),
        "ple_norm_g": 1.0 + nrm(ks[24], (L, D_MODEL), 0.02),
        "ple_gate_norm_g": 1.0 + nrm(ks[25], (L, D_MODEL), 0.02),
        "ple_gate_w": nrm(ks[26], (L, D_MODEL, D_MODEL), D_MODEL ** -0.5),
        "ple_gate_b": nrm(ks[27], (L, D_MODEL), 0.02),
    }

def reference(x, p, attn_norm_g, w_in, shift_mu, w0, w2, a0, a2, g2, k_k, k_a, r_k,
              lnx_g, lnx_b, q_norm_g, k_norm_g, fgate_b, w_out, ffn_norm_g, w_gate,
              w_up, w_down, ple_proj, ple_norm_g, ple_gate_norm_g, ple_gate_w, ple_gate_b):
    h = x
    for i in range(DEPTH):
        u = rmsnorm(h, attn_norm_g[i]) @ w_in[i]
        u_rwkv, u_fox = u[..., :RWKV_COLS], u[..., RWKV_COLS:]
        y_rwkv = rwkv7_mix(u_rwkv, shift_mu[i], w0[i], w2[i], a0[i], a2[i], g2[i],
                           k_k[i], k_a[i], r_k[i], lnx_g[i], lnx_b[i])
        y_fox = fox_mix(u_fox, q_norm_g[i], k_norm_g[i], fgate_b[i])
        y = jnp.concatenate([y_rwkv, y_fox], axis=-1).astype(h.dtype)
        h = h + y @ w_out[i]
        hn = rmsnorm(h, ffn_norm_g[i])
        h = h + (jax.nn.silu(hn @ w_gate[i]) * (hn @ w_up[i])) @ w_down[i]
        e = rmsnorm(p[i] @ ple_proj[i], ple_norm_g[i])
        gate = jax.nn.sigmoid(rmsnorm(h, ple_gate_norm_g[i]) @ ple_gate_w[i] + ple_gate_b[i])
        h = h + gate * e
    return h


_drawn_inputs = setup_inputs


def setup_inputs(seed=0):
    import zlib

    import numpy as np

    out = dict(_drawn_inputs(seed))
    spreads = {}
    factors = {'attn_norm_g': 3.745,
     'w2': 6.316,
     'a0': 3.718,
     'k_k': 24.826,
     'k_a': 2.961,
     'lnx_g': 46.332,
     'lnx_b': 49.682,
     'q_norm_g': 8.0,
     'k_norm_g': 8.0,
     'ffn_norm_g': 4.532,
     'ple_norm_g': 56.64,
     'ple_gate_norm_g': 64.0,
     'ple_gate_b': 64.0}
    for name, (base, spread) in spreads.items():
        noise = np.random.default_rng([zlib.crc32(name.encode()), seed]).standard_normal(out[name].shape)
        drawn = base * np.exp(spread * noise) if base else spread * noise
        out[name] = __import__('jax').numpy.asarray(drawn.astype(out[name].dtype))
    for name, factor in factors.items():
        out[name] = (out[name] * factor).astype(out[name].dtype)
    return out
```

```python
from contextlib import ExitStack
import math

import concourse.bass as bass
from concourse import mybir

F32 = mybir.dt.float32
F32R = mybir.dt.float32r
BF16 = mybir.dt.bfloat16
U32 = mybir.dt.uint32
ALU = mybir.AluOpType
ACT = mybir.ActivationFunctionType
AX = mybir.AxisListType

P = 128
SEQ = 512
D_MODEL = 2048
KT = D_MODEL // P
HALF = KT // 2
TT = SEQ // P
HD = 64
GROUPS = 4
GH = 4
LORA = 96
LORA_SLABS = 4
GROUP_SLABS = 12
IN_SLABS = LORA_SLABS + GROUPS * GROUP_SLABS
OUT_SLABS = D_MODEL // P
D_FF = 5632
CHUNKS = 4
CF = D_FF // P // CHUNKS
DOWN_HALVES = (6, CF - 6)
N_OUT = IN_SLABS
N_FFN = N_OUT + OUT_SLABS
CHUNK_SLABS = 2 * CF + OUT_SLABS
N_PROJ = N_FFN + CHUNKS * CHUNK_SLABS
PROJ_SLABS = 2
PROJ_TILES = 8
N_GATE = N_PROJ + PROJ_SLABS
TILE_GATE = N_PROJ + PROJ_SLABS * PROJ_TILES
LEVELS = 6
STAGES = 24
NORM_X, NORM_FFN, NORM_GATE, NORM_E = 1, 2, 3, 4
DECAY = math.exp(-0.5)
RMS_EPS, GN_EPS = 1e-6, 64e-5
C_ID, C_ONE, C_BLK, C_STRICT, C_INCL, C_LEVEL, C_COL = [P * i for i in (0, 1, 2, 3, 4, 5, 5 + LEVELS + 1)]
PAR = {}
for _name, _width in (("attn_g", 16), ("ffn_g", 16), ("gate_g", 16), ("ple_g", 16), ("gate_b", 16),
                      ("mu", 4), ("f_bias", 1), ("q_g", 1), ("k_g", 1)):
    PAR[_name] = (sum(w for _, w in PAR.values()), _width)
N_PAR = sum(w for _, w in PAR.values())
MU_K, MU_R, MU_V, K_K, K_A, R_K, W0, A0, LN_G, LN_B = range(10)
NG_PAR = 10


def after(eng, sem, value):
    if not (isinstance(value, int) and value <= 0):
        eng.wait_ge(sem, value)


def layer(nc, d):
    sems = {}

    def S(name):
        if name not in sems:
            sems[name] = nc.alloc_semaphore(name)
        return sems[name]

    scratch = {}

    def own_wait(eng, place=1):
        t = scratch[eng.engine]
        if eng.engine == mybir.EngineType.DVE:
            nc.vector.memset(t[:, place:place + 1], 0.0)
        elif eng.engine == mybir.EngineType.Pool:
            nc.gpsimd.tensor_tensor(t[:, place:place + 1], t[:, 0:1], t[:, 0:1], ALU.add)
        else:
            nc.scalar.activation(t[:, 1:2], t[:, 0:1], ACT.Copy)

    f32 = lambda name, shape: nc.dram_tensor(name, shape, F32)
    y_dram = f32("y_scratch", [KT, P, SEQ]).ap()
    c_dram = f32("c_scratch", [2, 16, SEQ]).ap()

    at = [(nc.sbuf_base + 63) // 64 * 64]

    def sb(name, shape, dt=F32):
        size = math.prod(shape[1:]) * (2 if dt == BF16 else 4)
        t = nc.alloc_sbuf_tensor_at(name, shape, dt, offset=at[0])
        at[0] += (size + 31) // 32 * 32
        assert at[0] <= nc.sbuf_usable_end, (name, at[0], nc.sbuf_usable_end)
        return t

    raw = sb("raw", [P, 2, HALF * P])
    w_hi = sb("w_hi", [P, 4, HALF * P], F32R)
    w_lo = sb("w_lo", [P, 4, HALF * P], F32R)
    par = sb("par", [P, N_PAR])
    ccol = sb("ccol", [P, 8])
    ones = sb("ones", [P, P])
    for _e, _n in ((mybir.EngineType.DVE, "dve"), (mybir.EngineType.Pool, "pool"), (mybir.EngineType.Activation, "act")):
        scratch[_e] = sb("scratch_" + _n, [P, 8])
    qg8 = sb("qg8", [P, 1])
    first = at[0]
    in_hi = sb("in_hi", [P, KT, SEQ], F32R)
    in_lo = sb("in_lo", [P, KT, SEQ], F32R)
    shared = at[0]
    at[0] = first
    act_hi = sb("act_hi", [P, CF, SEQ], F32R)
    act_lo = sb("act_lo", [P, CF, SEQ], F32R)
    gate_s = sb("gate_s", [P, SEQ])
    up_s = sb("up_s", [P, SEQ])
    silu_s = sb("silu_s", [P, SEQ])
    p_raw = sb("p_raw", [P, 2, SEQ])
    p_hi = sb("p_hi", [P, 2, SEQ], F32R)
    p_lo = sb("p_lo", [P, 2, SEQ], F32R)
    assert at[0] <= shared
    at[0] = first
    e_t = sb("e_t", [P, KT, SEQ])
    acc_e = sb("acc_e", [P, SEQ])
    rstd_e = sb("rstd_e", [P, SEQ])
    assert at[0] - first <= 2 * CF * SEQ * 4
    at[0] = shared
    h_t = sb("h_t", [P, KT, SEQ])
    hn_hi = sb("hn_hi", [P, KT, SEQ], F32R)
    hn_lo = sb("hn_lo", [P, KT, SEQ], F32R)
    sq_s = sb("sq_s", [P, SEQ])
    acc_h = sb("acc_h", [P, SEQ])
    rstd_h = sb("rstd_h", [P, SEQ])
    at[0] = shared
    consts = sb("consts", [P, C_COL + 8])
    id16 = sb("id16", [P, 2 * P], BF16)
    rstd_x = sb("rstd_x", [P, SEQ])
    acc_x = sb("acc_x", [P, 2, SEQ])
    tanh_w = sb("tanh_w", [P, SEQ])
    xa_t = sb("xa_t", [P, SEQ])
    sig_g = sb("sig_g", [P, 2, SEQ])
    work = at[0]
    x_raw = sb("x_raw", [P, KT, SEQ])
    sqx = sb("sqx", [P, 2, SEQ])
    at[0] = work
    g_par = sb("g_par", [P, 2, NG_PAR])
    w2a2 = sb("w2a2", [P, 2, 2 * P])
    g2_t = sb("g2_t", [P, 2, 2 * P])
    u_t = sb("u_t", [P, SEQ + 1])
    t1 = sb("t1", [P, SEQ])
    t2 = sb("t2", [P, SEQ])
    A_t = sb("A_t", [P, 2, SEQ])
    B_t = sb("B_t", [P, 2, SEQ])
    K_t = sb("K_t", [P, 2, SEQ])
    R_t = sb("R_t", [P, 2, SEQ])
    bonus = sb("bonus", [P, 2, SEQ])
    v_tok = sb("v_tok", [P, TT, 2 * P])
    state = sb("state", [P, 2, P])
    st_scale = sb("st_scale", [P, 2, TT])
    mid = sb("mid", [P, TT])
    q_aug = sb("q_aug", [P, GH, SEQ])
    k_aug = sb("k_aug", [P, GH, SEQ])
    fv_tok = sb("fv_tok", [P, TT, 2 * P])
    small = sb("small", [P, 64])
    stats_t = sb("stats_t", [P, GH, 6])
    o_t = sb("o_t", [P, 2, SEQ])
    overlay = at[0]
    sg_t = sb("sg_t", [P, SEQ])
    a_t = sb("a_t", [P, SEQ])
    d_t = sb("d_t", [P, SEQ])
    pi_t = sb("pi_t", [P, SEQ])
    probs = sb("probs", [P, 2, SEQ])
    probs_T = sb("probs_T", [P, TT, SEQ])
    at[0] = overlay + 4 * 4 * SEQ
    cf = sb("cf", [P, 2, SEQ])
    at[0] = overlay
    LM = sb("LM", [P, 2, 2, 2, P])
    RM = sb("RM", [P, 2, 2, 2, P])
    LTm = sb("LTm", [P, 2, GH, P])
    T_inv = sb("T_inv", [P, GH, P])
    T_invT = sb("T_invT", [P, GH, P])
    X_t = sb("X_t", [P, GH, P])
    bk_tok = sb("bk_tok", [P, 4, P])
    R0_t = sb("R0_t", [P, GH * HD])
    U_t = sb("U_t", [P, GH * HD])
    Yn_t = R0_t

    psum = [nc.alloc_psum_tensor(f"bank{i}", [P, SEQ], F32) for i in range(8)]
    aux, b3, b4, b5, b6, b7 = psum[2:]

    def gain_of(name):
        a, w = PAR[name]
        return par[:, a:a + w]

    def const(c, n=P):
        return consts[:, c:c + n]

    def over_heads(c):
        return consts[:, c:c + P].unsqueeze(1).to_broadcast([P, GH, P])

    by_parity = lambda ap: ap.rearrange("p (a f) c -> p a f c", a=2)

    CB_RMS, CB_GN, CB_KK, CB_ZERO = range(4)
    cb = lambda i: ccol[:, i:i + 1]

    raw_landed = [S("raw_landed_first_half"), S("raw_landed_second_half")]
    hi_ready, lo_ready, weights_used = S("hi_ready"), S("lo_ready"), S("weights_used")
    tile_evacuated = S("tile_evacuated")

    ring_slots = lambda n_par, half: 2 * n_par + half

    def load_slab(sp, n, src, cols=(HALF * P, HALF * P), start=0):
        for half in range(2):
            after(sp, lo_ready, 2 * n + half - 1)
            sp.dma_start(raw[:, half, 0:cols[half]], src[:, sum(cols[:half]):sum(cols[:half + 1])]
                         ).then_inc(raw_landed[half], 16)

    def round_slab(act, n, par2, cols=(HALF * P, HALF * P)):
        for half in range(2):
            act.wait_ge(raw_landed[half], 16 * (n + 1))
            after(act, weights_used, 2 * n + half - 3)
            nc.scalar.activation(w_hi[:, ring_slots(par2, half), 0:cols[half]], raw[:, half, 0:cols[half]],
                                 ACT.Copy).then_inc(hi_ready, 1)

    def subtract_slab(dve, n, par2, cols=(HALF * P, HALF * P)):
        for half in range(2):
            dve.wait_ge(hi_ready, 2 * n + half + 1)
            s = ring_slots(par2, half)
            nc.vector.tensor_tensor(w_lo[:, s, 0:cols[half]], raw[:, half, 0:cols[half]],
                                    w_hi[:, s, 0:cols[half]].bitcast(F32), ALU.subtract).then_inc(lo_ready, 1)

    def three_products(out, s, col, x_hi, x_lo, start, stop):
        w_h, w_l = w_hi[:, s, col:col + P], w_lo[:, s, col:col + P]
        nc.tensor.matmul(out, w_h, x_hi, start=start, stop=False, skip_group_check=True)
        nc.tensor.matmul(out, w_h, x_lo, start=False, stop=False, skip_group_check=True)
        return nc.tensor.matmul(out, w_l, x_hi, start=False, stop=stop, skip_group_check=True)

    def multiply_slab(pe, n, par2, x_hi, x_lo, kts=(HALF, HALF), side=None, input_ready=None):
        after(pe, tile_evacuated, n - 1)
        kt = 0
        for half in range(2):
            pe.wait_ge(lo_ready, 2 * n + half + 1)
            for k in range(kts[half]):
                if side is not None:
                    side(kt)
                if input_ready is not None:
                    input_ready(kt)
                last = three_products(psum[par2][:], ring_slots(par2, half), k * P, x_hi[:, kt, :], x_lo[:, kt, :],
                                      kt == 0, kt == sum(kts) - 1)
                kt += 1
            last.then_inc(weights_used, 1)

    bank_b = [b3, b4, b5, b6, b7]
    s_bank = [b3, b4]
    pt_bank = [b5, b6]
    hp = lambda j: slice(HD * (j % 2), HD * (j % 2) + HD)
    tok = lambda tt: slice(tt * P, (tt + 1) * P)

    def pe_rwkv_prep(pe, s, kt, g):
        ft, kind = s // 3, s % 3
        f = 2 * g + ft
        if kind == 0 and kt == 8:
            if ft == 0:
                pe.wait_ge(S("g_weights_landed"), 32 * (g + 1))
                pe.wait_ge(S("tanh_ready"), 1)
                pe.wait_ge(S("xa_ready"), 1)
                if not (isinstance(g, int) and g == 0):
                    pe.wait_ge(S("y_rwkv_ready"), 2 * g)
                else:
                    pe.wait_ge(S("norm_ready"), NORM_X)
            else:
                pe.wait_ge(S("v_tok_ready"), f)
            nc.tensor.matmul(aux[:], w2a2[0:LORA, 0, tok(ft)], tanh_w[0:LORA, :], start=True, stop=True
                             ).then_inc(S("z_done"), 1)
        if kind == 0 and kt == 10:
            pe.wait_ge(S("sigmoid_z_ready"), f + 1)
            nc.tensor.matmul(aux[:], w2a2[0:LORA, 1, tok(ft)], xa_t[0:LORA, :], start=True, stop=True
                             ).then_inc(S("a_done"), 1)
        if kind == 1 and kt == 4:
            pe.wait_ge(S("k_square_ready"), f + 1)
            pe.wait_ge(S("a_ready"), f + 1)
            nc.tensor.matmul(aux[:], const(C_BLK), t1[:], start=True, stop=True).then_inc(S("k_sum_done"), 1)
        if kind == 2 and kt == 4:
            pe.wait_ge(S("rk_ready"), f + 1)
            pe.wait_ge(S("k_sum_ready"), f + 1)
            nc.tensor.matmul(aux[:], const(C_BLK), t1[:], start=True, stop=True).then_inc(S("bonus_done"), 1)
        if s == 3 and kt == 4:
            pe_values(pe, 2 * g)

    def pe_values(pe, f):
        pe.wait_ge(S("v_mixed"), f + 1)
        pe.wait_ge(S("bonus_ready"), f + 1)
        for tt in range(TT):
            last = nc.tensor.transpose(aux[:, tok(tt)], t2[:, tok(tt)], const(C_ID))
        last.then_inc(S("v_turned"), 1)

    def pe_fox_values(pe, g, ft):
        pe.wait_ge(tile_evacuated, LORA_SLABS + GROUP_SLABS * g + GROUP_SLABS - 1 + ft)
        for tt in range(TT):
            last = nc.tensor.transpose(aux[:, tok(tt)], u_t[:, 1 + tt * P:1 + (tt + 1) * P], const(C_ID))
        last.then_inc(S("fox_v_turned"), 1)

    def pe_fox_prep(pe, s, kt, g):
        if kt != 4 or s < 6:
            return
        if s == 6:
            pe_values(pe, 2 * g + 1)
            return
        c = s - 7
        if c < 4:
            pe.wait_ge(S("fox_square_ready"), 4 * g + c + 1)
            if c == 0:
                pe.wait_ge(S("v_tok_ready"), 2 * g + 2)
            else:
                pe.wait_ge(S("fox_rstd_ready"), 4 * g + c)
            nc.tensor.matmul(aux[:], const(C_BLK), t1[:], start=True, stop=True).then_inc(S("fox_sum_done"), 1)
        else:
            pe.wait_ge(S("fox_rstd_ready"), 4 * g + 4)
            pe_fox_values(pe, g, 0)

    def pe_finish(pe, s, kt, gp):
        if s == 0 and kt == 2:
            pe.wait_ge(S("fox_v_tok_ready"), 2 * gp + 1)
            pe_fox_values(pe, gp, 1)
        if s == 0 and kt in (4, 6):
            ft = (kt - 4) // 2
            if ft == 0:
                pe.wait_ge(S("g2_landed"), 16 * (gp + 1))
                pe.wait_ge(S("sig_g_ready"), 2)
                pe.wait_ge(S("fox_v_tok_ready"), 2 * gp + 2)
            else:
                pe.wait_ge(S("y_rwkv_ready"), 2 * gp + 1)
            for k in range(2):
                last = nc.tensor.matmul(aux[:], g2_t[:, k, tok(ft)], sig_g[:, k, :], start=k == 0, stop=k == 1)
            last.then_inc(S("g_done"), 1)

    def attention_step(s, kt):
        st = 16 * s + kt
        return st // 6, st % 6

    def pe_attention(pe, s, kt, gp):
        q, part = attention_step(s, kt)
        j, i = q // TT, q % TT
        if part == 0:
            if q == 0:
                pe.wait_ge(S("fox_qk_ready"), 4 * gp + 4)
                pe.wait_ge(S("c_rows_landed"), 32 * (gp + 1))
                pe.wait_ge(S("y_norm_ready"), 4 * gp + 4)
            if q == 1:
                pe.wait_ge(S("X_ready"), LEVELS * (4 * gp + 4))
                pe.wait_ge(S("state_ready"), 4 * gp + 4)
            if q >= 2:
                pe.wait_ge(S("probs_ready"), 16 * gp + q - 1)
            n = (i + 1) * P
            bank = s_bank[q % 2]
            nc.tensor.matmul(bank[:, 0:n], q_aug[0:HD + 2, j, tok(i)], k_aug[0:HD + 2, j, 0:n],
                             start=True, stop=False, skip_group_check=True)
            nc.tensor.matmul(bank[:, tok(i)], id16[:, 0:P], id16[:, P:2 * P],
                             start=False, stop=True, skip_group_check=True).then_inc(S("scores_done"), 1)
        if part == 4:
            pe.wait_ge(S("probs_normed"), 16 * gp + q + 1)
            if q == 0:
                pe.wait_ge(S("y_turned_ready"), 4 * gp + 4)
            if q == 1:
                pe.wait_ge(S("TT_ready"), LEVELS * (4 * gp + 4))
            if q >= 2:
                pe.wait_ge(S("probs_T_ready"), 16 * gp + q - 1)
            for kb in range(i + 1):
                last = nc.tensor.transpose(pt_bank[q % 2][:, tok(kb)], probs[:, q % 2, tok(kb)], const(C_ID))
            last.then_inc(S("probs_turned"), 1)
        if part == 5 and i == TT - 1:
            pe.wait_ge(S("probs_T_ready"), 16 * gp + q + 1)
            if j == 0:
                pe.wait_ge(S("fox_v_tok_ready"), 2 * gp + 2)
                pe.wait_ge(S("U_ready"), 4 * gp + 4)
            if j == 2:
                pe.wait_ge(S("o_ready"), 2 * gp + 1)
            for kb in range(TT):
                last = nc.tensor.matmul(b7[hp(j), kb * P:SEQ], fv_tok[:, kb, j * HD:(j + 1) * HD],
                                        probs_T[:, kb, kb * P:SEQ], start=kb == 0, stop=kb == TT - 1,
                                        skip_group_check=True)
            last.then_inc(S("pv_done"), 1)

    def stage_of(s, kt):
        st = 16 * (s - 6) + kt
        return st // STAGES, st % STAGES

    place = lambda j: 2 * (j % 2) + j // 2

    def grams(bank, rhs, tt, odd):
        for n, lhs in enumerate((B_t, K_t)):
            for ft in range(2):
                last = nc.tensor.matmul(bank[:, tok(2 * n + ft)], lhs[hp(odd), ft, tok(tt)],
                                        rhs[hp(odd), ft, tok(tt)], start=True, stop=True, skip_group_check=True)
        return last

    def pe_recurrence(pe, s, kt, g):
        tt, k = stage_of(s, kt)
        b = 4 * g + tt
        later = not (isinstance(g, int) and g == 0)
        if k == 0:
            pe.wait_ge(S("K_ready"), 2 * g + 2)
            if tt == 0:
                if later:
                    pe.wait_ge(S("probs_ready"), 16 * g)
            else:
                pe.wait_ge(S("y_norm_ready"), b)
            for n, (src, ft) in enumerate(((B_t, 0), (B_t, 1), (K_t, 0), (K_t, 1))):
                last = nc.tensor.transpose(b3[:, tok(n)], src[:, ft, tok(tt)], const(C_ID))
            last.then_inc(S("bk_turned"), 1)
        if k == 1:
            if tt > 0:
                pe.wait_ge(S("state_ready"), b + 1)
            grams(b4, A_t, tt, 0).then_inc(S("LM_done"), 1)
        if k == 2:
            if tt == 0 and later:
                pe.wait_ge(S("probs_T_ready"), 16 * g)
            if tt > 0:
                pe.wait_ge(S("y_turned_ready"), b)
            grams(b5, A_t, tt, 1).then_inc(S("LM_done"), 1)
        if k == 3:
            pe.wait_ge(S("R_ready"), 2 * g + 2)
            grams(b6, R_t, tt, 0).then_inc(S("RM_done"), 1)
        if k == 4:
            if tt == 0 and later:
                pe.wait_ge(S("o_ready"), 2 * g)
            grams(b7, R_t, tt, 1).then_inc(S("RM_done"), 1)
        if k == 5:
            pe.wait_ge(S("TT0_ready"), b + 1)
            pe.wait_ge(S("bk_tok_ready"), b + 1)
            for j in range(GH):
                last = nc.tensor.transpose(b3[:, tok(j)], T_invT[:, j, :], const(C_ID))
            last.then_inc(S("T0_done"), 1)
        if 6 <= k < 6 + 2 * LEVELS:
            m, part = (k - 6) // 2 + 1, (k - 6) % 2
            if part == 0:
                pe.wait_ge(S("LT_level_ready"), LEVELS * b + m)
                pe.wait_ge(S("T_ready"), LEVELS * b + m)
                for j in range(GH):
                    last = nc.tensor.matmul(b4[:, tok(j)], LTm[:, (m - 1) % 2, j, :], T_inv[:, j, :],
                                            start=True, stop=True, skip_group_check=True)
                last.then_inc(S("X_done"), 1)
            else:
                pe.wait_ge(S("X_ready"), LEVELS * b + m)
                if m > 1:
                    pe.wait_ge(S("TT_ready"), LEVELS * b + m - 1)
                else:
                    pe.wait_ge(S("LM_ready"), 2 * b + 2)
                    pe.wait_ge(S("RM_ready"), 2 * b + 1)
                if m < LEVELS:
                    for j in range(GH):
                        last = nc.tensor.matmul(b5[:, tok(j)], T_invT[:, j, :], X_t[:, j, :],
                                                start=True, stop=True, skip_group_check=True)
                    last.then_inc(S("dT_done"), 1)
                for j in range(GH):
                    last = nc.tensor.matmul(b6[:, tok(j)], X_t[:, j, :], T_invT[:, j, :],
                                            start=True, stop=True, skip_group_check=True)
                last.then_inc(S("dTT_done"), 1)
        if k == 18:
            pe.wait_ge(S("RM_ready"), 2 * b + 2)
            pe.wait_ge(S("v_tok_ready"), 2 * g + 2)
            pe.wait_ge(S("state_ready"), b + 1)
            for ft in range(2):
                nc.tensor.matmul(b7[:, tok(ft)], A_t[:, ft, tok(tt)], state[:, ft, :],
                                 start=True, stop=False, skip_group_check=True)
                for j in (2 * ft, 2 * ft + 1):
                    v = slice(j * HD, (j + 1) * HD)
                    last = nc.tensor.matmul(b7[:, v], LM[:, j % 2, 1, ft, :], v_tok[:, tt, v],
                                            start=False, stop=True, skip_group_check=True)
            last.then_inc(S("R0_done"), 1)
        if k == 19:
            pe.wait_ge(S("R0_ready"), b + 1)
            pe.wait_ge(S("TT_ready"), LEVELS * b + LEVELS)
            for j in range(GH):
                last = nc.tensor.matmul(b7[:, GH * HD + j * HD:GH * HD + (j + 1) * HD], T_invT[:, place(j), :],
                                        R0_t[:, j * HD:(j + 1) * HD], start=True, stop=True, skip_group_check=True)
            last.then_inc(S("U_done"), 1)
        if k == 20:
            pe.wait_ge(S("U_ready"), b + 1)
            for ft in range(2):
                nc.tensor.matmul(b3[:, tok(ft)], R_t[:, ft, tok(tt)], state[:, ft, :],
                                 start=True, stop=False, skip_group_check=True)
                for j in (2 * ft, 2 * ft + 1):
                    v = slice(j * HD, (j + 1) * HD)
                    nc.tensor.matmul(b3[:, v], RM[:, j % 2, 0, ft, :], U_t[:, v], start=False, stop=False,
                                     skip_group_check=True)
                    last = nc.tensor.matmul(b3[:, v], RM[:, j % 2, 1, ft, :], v_tok[:, tt, v], start=False,
                                            stop=True, skip_group_check=True)
            last.then_inc(S("Y_done"), 1)
            if tt < TT - 1:
                for ft in range(2):
                    nc.tensor.matmul(b4[:, tok(ft)], bk_tok[:, ft, :], U_t[:, tok(ft)],
                                     start=True, stop=False, skip_group_check=True)
                    last = nc.tensor.matmul(b4[:, tok(ft)], bk_tok[:, 2 + ft, :], v_tok[:, tt, tok(ft)],
                                            start=False, stop=True, skip_group_check=True)
                last.then_inc(S("state_step_done"), 1)
        if k == 22:
            pe.wait_ge(S("y_norm_ready"), b + 1)
            for ft in range(2):
                last = nc.tensor.transpose(b5[:, tok(ft)], Yn_t[:, tok(ft)], const(C_ID))
            last.then_inc(S("y_turned"), 1)

    def act_rwkv_prep(act, s, kt, g):
        ft, kind = s // 3, s % 3
        f = 2 * g + ft
        gp_col = lambda c: g_par[:, ft, c:c + 1]
        if kind == 0 and kt == 8:
            act.wait_ge(S("z_done"), f + 1)
            act.wait_ge(S("g_par_landed"), 16 * (g + 1))
            nc.scalar.activation(sg_t[:], aux[:], ACT.Sigmoid, bias=gp_col(W0)).then_inc(S("sigmoid_z_ready"), 1)
        if kind == 0 and kt == 10:
            act.wait_ge(S("a_done"), f + 1)
            nc.scalar.activation(a_t[:], aux[:], ACT.Sigmoid, bias=gp_col(A0)).then_inc(S("a_ready"), 1)
        if kind == 0 and kt == 12:
            act.wait_ge(S("d_ready"), f + 1)
            act.wait_ge(S("st_exponent_ready"), f + 1)
            act.wait_ge(S("d_prev_ready"), f + 1)
            nc.scalar.activation(pi_t[:], d_t[:], ACT.Exp, scale=DECAY).then_inc(S("inverse_decay_ready"), 1)
            act.wait_ge(S("inverse_decay_ready"), f + 1)
            nc.scalar.activation(d_t[:], d_t[:], ACT.Exp, scale=-DECAY)
            nc.scalar.activation(sg_t[:], sg_t[:], ACT.Exp, scale=-DECAY)
            nc.scalar.activation(st_scale[:, ft, 0:TT - 1], small[:, 0:TT - 1], ACT.Exp,
                                 scale=-DECAY).then_inc(S("decays_ready"), 1)
        if kind == 1 and kt == 2:
            act.wait_ge(S("k_mixed"), f + 1)
            nc.scalar.activation(t1[:], t2[:], ACT.Square, scale=gp_col(K_K)).then_inc(S("k_square_ready"), 1)
        if kind == 1 and kt == 5:
            act.wait_ge(S("k_sum_ready"), f + 1)
            nc.scalar.activation(t1[:], t1[:], ACT.Ln, scale=2.0 ** 16).then_inc(S("k_log_ready"), 1)
            act.wait_ge(S("k_log_ready"), f + 1)
            nc.scalar.activation(t1[:], t1[:], ACT.Exp, scale=-0.5, bias=cb(CB_KK)).then_inc(S("k_rnorm_ready"), 1)
        if kind == 2 and kt == 5:
            act.wait_ge(S("bonus_done"), f + 1)
            if not (isinstance(g, int) and g == 0):
                act.wait_ge(S("y_plus_bonus"), 2 * g)
            nc.scalar.activation(bonus[:, ft, :], aux[:], ACT.Copy).then_inc(S("bonus_ready"), 1)
        if s == 3 and kt == 5:
            act_values(act, g, 0)

    def act_values(act, g, ft):
        act.wait_ge(S("v_turned"), 2 * g + ft + 1)
        nc.scalar.activation(v_tok[:, :, tok(ft)], aux[:].rearrange("p (t c) -> p t c", t=TT), ACT.Copy
                             ).then_inc(S("v_tok_ready"), 1)

    def act_fox_values(act, gf, ft):
        act.wait_ge(S("fox_v_turned"), gf + 1)
        nc.scalar.activation(fv_tok[:, :, tok(ft)], aux[:].rearrange("p (t c) -> p t c", t=TT), ACT.Copy
                             ).then_inc(S("fox_v_tok_ready"), 1)

    def act_fox_prep(act, s, kt, g):
        if s == 6 and kt == 5:
            act_values(act, g, 1)
        c = s - 7
        if 0 <= c < 4 and kt == 2:
            act.wait_ge(tile_evacuated, LORA_SLABS + GROUP_SLABS * g + s)
            nc.scalar.activation(t1[:], u_t[:, 1:SEQ + 1], ACT.Square).then_inc(S("fox_square_ready"), 1)
        if 0 <= c < 4 and kt == 5:
            act.wait_ge(S("fox_sum_done"), 4 * g + c + 1)
            nc.scalar.activation(t2[:], aux[:], ACT.Ln, scale=1.0 / HD, bias=cb(CB_RMS)
                                 ).then_inc(S("fox_log_ready"), 1)
            act.wait_ge(S("fox_log_ready"), 4 * g + c + 1)
            nc.scalar.activation(t2[:], t2[:], ACT.Exp, scale=-0.5).then_inc(S("fox_rstd_ready"), 1)
        if c == 4 and kt == 5:
            act_fox_values(act, 2 * g, 0)

    def act_finish(act, s, kt, gp):
        if s == 0 and kt == 2:
            act_fox_values(act, 2 * gp + 1, 1)

    def act_attention(act, s, kt, gp):
        q, part = attention_step(s, kt)
        j, i = q // TT, q % TT
        n = (i + 1) * P
        if part == 1:
            act.wait_ge(S("max_ready"), 16 * gp + q + 1)
            if q >= 2:
                act.wait_ge(S("probs_turned"), 16 * gp + q - 1)
            nc.scalar.activation(probs[:, q % 2, 0:n], s_bank[q % 2][:, 0:n], ACT.Exp,
                                 bias=small[:, 8 + q % 2:9 + q % 2], accum_out=small[:, 10 + q % 2:11 + q % 2]
                                 ).then_inc(S("probs_ready"), 1)
        if part == 4:
            act.wait_ge(S("probs_turned"), 16 * gp + q + 1)
            if i == 0 and j > 0:
                act.wait_ge(S("pv_done"), 4 * gp + j)
            nc.scalar.activation(probs_T[:, 0:i + 1, tok(i)],
                                 pt_bank[q % 2][:, 0:n].rearrange("p (k c) -> p k c", c=P), ACT.Copy
                                 ).then_inc(S("probs_T_ready"), 1)

    def act_recurrence(act, s, kt, g):
        tt, k = stage_of(s, kt)
        b = 4 * g + tt
        v4 = lambda bank: bank[:].rearrange("p (h c) -> p h c", h=GH)
        if k == 0:
            act.wait_ge(S("bk_turned"), b + 1)
            if tt > 0:
                act.wait_ge(S("state_step_done"), 3 * g + tt)
            nc.scalar.activation(bk_tok[:], v4(b3), ACT.Copy).then_inc(S("bk_tok_ready"), 1)
        if k == 5:
            act.wait_ge(S("T0_done"), b + 1)
            nc.scalar.activation(T_inv[:], v4(b3), ACT.Copy).then_inc(S("T_ready"), 1)
        if 6 <= k < 6 + 2 * LEVELS and (k - 6) % 2 == 0:
            m = (k - 6) // 2 + 1
            act.wait_ge(S("X_done"), LEVELS * b + m)
            nc.scalar.activation(X_t[:], v4(b4), ACT.Copy).then_inc(S("X_ready"), 1)
        if k == 18:
            act.wait_ge(S("R0_done"), b + 1)
            nc.scalar.activation(R0_t[:], b7[:, 0:GH * HD], ACT.Copy).then_inc(S("R0_ready"), 1)
        if k == 19:
            act.wait_ge(S("U_done"), b + 1)
            nc.scalar.activation(U_t[:], b7[:, GH * HD:2 * GH * HD], ACT.Copy).then_inc(S("U_ready"), 1)
        if k == 20:
            act.wait_ge(S("y_stats_ready"), b + 1)
            nc.scalar.activation(small[:, 20:24], small[:, 40:48:2], ACT.Ln, bias=cb(CB_GN)
                                 ).then_inc(S("y_log_ready"), 1)
            act.wait_ge(S("y_log_ready"), b + 1)
            nc.scalar.activation(small[:, 24:28], small[:, 20:24], ACT.Exp, scale=-0.5).then_inc(S("y_rstd_ready"), 1)
        if k == 22:
            act.wait_ge(S("y_turned"), b + 1)
            for ft in range(2):
                ins = nc.scalar.activation(R_t[:, ft, tok(tt)], b5[:, tok(ft)], ACT.Identity,
                                           scale=g_par[:, ft, LN_G:LN_G + 1], bias=g_par[:, ft, LN_B:LN_B + 1])
            ins.then_inc(S("y_turned_ready"), 1)

    def evacuate(dve, n, par2):
        dve.wait_ge(weights_used, 2 * n + 2)
        return nc.vector.tensor_tensor(u_t[:, 1:SEQ + 1], psum[par2][:], rstd_x[:], ALU.mult)

    def dve_arrival_rwkv(dve, s, g):
        n = LORA_SLABS + GROUP_SLABS * g + s - 1
        ft, kind = (s - 1) // 3, (s - 1) % 3
        f = 2 * g + ft
        a = 6 * g + s - 1
        gp_col = lambda c: g_par[:, ft, c:c + 1]
        if s == 1 and isinstance(g, int) and g == 0:
            dve.wait_ge(S("lora_mixed"), LORA_SLABS - 1)
        if s == 1 and not (isinstance(g, int) and g == 0):
            dve.wait_ge(S("fox_v_turned"), 2 * g)
        evacuate(dve, n, (s - 1) % 2).then_inc(tile_evacuated, 1)
        if s == 1:
            dve.wait_ge(S("g_par_landed"), 16 * (g + 1))
        dve.wait_ge(S("shift_ready"), LORA_SLABS + a + 1)
        if kind == 0:
            if ft == 1:
                dve.wait_ge(S("v_turned"), f)
            after(dve, S("bonus_v_ready"), f)
            nc.vector.scalar_tensor_tensor(out=t2[:], in0=t1[:], scalar=gp_col(MU_K), in1=u_t[:, 1:SEQ + 1],
                                           op0=ALU.mult, op1=ALU.add).then_inc(S("k_mixed"), 1)
        if kind == 1:
            if ft == 0 and not (isinstance(g, int) and g == 0):
                dve.wait_ge(S("y_rwkv_stored"), 32 * g)
            nc.vector.scalar_tensor_tensor(out=R_t[:, ft, :], in0=t1[:], scalar=gp_col(MU_R),
                                           in1=u_t[:, 1:SEQ + 1], op0=ALU.mult, op1=ALU.add
                                           ).then_inc(S("r_mixed"), 1)
            dve.wait_ge(S("r_mixed"), f + 1)
            nc.vector.scalar_tensor_tensor(out=t1[:], in0=R_t[:, ft, :], scalar=gp_col(R_K), in1=t2[:],
                                           op0=ALU.mult, op1=ALU.mult).then_inc(S("rk_ready"), 1)
            dve.wait_ge(S("rk_ready"), f + 1)
            nc.vector.tensor_tensor(R_t[:, ft, :], R_t[:, ft, :], d_t[:], ALU.mult).then_inc(S("R_ready"), 1)
        if kind == 2:
            nc.vector.scalar_tensor_tensor(out=t2[:], in0=t1[:], scalar=gp_col(MU_V), in1=u_t[:, 1:SEQ + 1],
                                           op0=ALU.mult, op1=ALU.add).then_inc(S("v_mixed"), 1)
            dve.wait_ge(S("v_mixed"), f + 1)
            dve.wait_ge(S("bonus_ready"), f + 1)
            nc.vector.tensor_tensor(bonus[:, ft, :], bonus[:, ft, :], t2[:], ALU.mult).then_inc(S("bonus_v_ready"), 1)

    def dve_rwkv_prep(dve, s, kt, g):
        ft, kind = s // 3, s % 3
        f = 2 * g + ft
        gp_col = lambda c: g_par[:, ft, c:c + 1]
        if kind == 0 and kt == 9:
            dve.wait_ge(S("sigmoid_z_ready"), f + 1)
            after(dve, S("R_ready"), f)
            for tt in range(TT):
                ins = nc.vector.tensor_tensor_scan(d_t[:, tok(tt)], ones[:], sg_t[:, tok(tt)], 0.0, ALU.mult, ALU.add)
            ins.then_inc(S("scan_step"), 1)
            dve.wait_ge(S("scan_step"), 2 * f + 1)
            d3 = d_t[:].rearrange("p (t c) -> p t c", t=TT)
            nc.vector.tensor_copy(mid[:], d3[:, :, P // 2 - 1]).then_inc(S("scan_step"), 1)
            dve.wait_ge(S("scan_step"), 2 * f + 2)
            nc.vector.tensor_tensor(d3, d3, mid[:].unsqueeze(2).to_broadcast([P, TT, P]), ALU.subtract
                                    ).then_inc(S("d_ready"), 1)
            dve.wait_ge(S("d_ready"), f + 1)
            nc.vector.tensor_tensor(small[:, 0:TT - 1], d3[:, 0:TT - 1, P - 1], mid[:, 1:TT], ALU.add
                                    ).then_inc(S("st_exponent_ready"), 1)
        if kind == 1 and kt == 4:
            dve.wait_ge(S("k_sum_done"), f + 1)
            nc.vector.tensor_scalar(t1[:], aux[:], 1e-24, None, ALU.max).then_inc(S("k_sum_ready"), 1)
        if kind == 1 and kt == 6:
            dve.wait_ge(S("k_rnorm_ready"), f + 1)
            dve.wait_ge(S("decays_ready"), f + 1)
            nc.vector.scalar_tensor_tensor(out=t1[:], in0=t2[:], scalar=gp_col(K_K), in1=t1[:],
                                           op0=ALU.mult, op1=ALU.mult).then_inc(S("key_step"), 1)
            dve.wait_ge(S("key_step"), 5 * f + 1)
            nc.vector.scalar_tensor_tensor(out=A_t[:, ft, :], in0=t1[:], scalar=-1.0, in1=sg_t[:],
                                           op0=ALU.mult, op1=ALU.mult).then_inc(S("key_step"), 1)
            dve.wait_ge(S("key_step"), 5 * f + 2)
            nc.vector.tensor_tensor(t1[:], t1[:], a_t[:], ALU.mult).then_inc(S("key_step"), 1)
            dve.wait_ge(S("key_step"), 5 * f + 3)
            nc.vector.tensor_tensor(B_t[:, ft, :], t1[:], pi_t[:], ALU.mult)
            nc.vector.tensor_scalar(a_t[:], a_t[:], -1.0, gp_col(K_A), ALU.add, ALU.mult
                                    ).then_inc(S("key_step"), 1)
            dve.wait_ge(S("key_step"), 5 * f + 4)
            nc.vector.scalar_tensor_tensor(out=t2[:], in0=a_t[:], scalar=1.0, in1=t2[:], op0=ALU.add, op1=ALU.mult
                                           ).then_inc(S("key_step"), 1)
            dve.wait_ge(S("key_step"), 5 * f + 5)
            nc.vector.tensor_tensor(K_t[:, ft, :], t2[:], pi_t[:], ALU.mult).then_inc(S("K_ready"), 1)

    def dve_arrival_fox(dve, s, g):
        n = LORA_SLABS + GROUP_SLABS * g + s - 1
        c = s - 7
        if c >= 1:
            if c <= 4:
                dve.wait_ge(S("fox_qk_ready"), 4 * g + c)
        if c == 5:
            dve.wait_ge(S("fox_v_turned"), 2 * g + 1)
        evacuate(dve, n, (s - 1) % 2).then_inc(tile_evacuated, 1)

    def dve_fox_prep(dve, s, kt, g):
        c = s - 7
        if 0 <= c < 4 and kt == 6:
            dve.wait_ge(S("fox_rstd_ready"), 4 * g + c + 1)
            dst, gain = (q_aug, qg8) if c < 2 else (k_aug, gain_of("k_g"))
            for hh in range(2):
                ps = slice(HD * hh, HD * hh + HD)
                ins = nc.vector.scalar_tensor_tensor(out=dst[0:HD, 2 * (c % 2) + hh, :], in0=u_t[ps, 1:SEQ + 1],
                                                     scalar=gain[ps, :], in1=t2[ps, :], op0=ALU.mult, op1=ALU.mult)
            ins.then_inc(S("fox_qk_ready"), 1)

    def dve_finish(dve, s, kt, gp):
        if s == 0 and kt in (4, 6):
            ft = (kt - 4) // 2
            dve.wait_ge(S("g_done"), 2 * gp + ft + 1)
            dve.wait_ge(S("y_plus_bonus"), 2 * gp + ft + 1)
            nc.vector.tensor_tensor(R_t[:, ft, :], R_t[:, ft, :], aux[:], ALU.mult).then_inc(S("y_rwkv_ready"), 1)

    def dve_attention(dve, s, kt, gp):
        q, part = attention_step(s, kt)
        j, i = q // TT, q % TT
        if part == 0:
            dve.wait_ge(S("scores_done"), 16 * gp + q + 1)
            nc.vector.tensor_reduce(small[:, 8 + q % 2:9 + q % 2], s_bank[q % 2][:, 0:(i + 1) * P], AX.X, ALU.max,
                                    negate=True).then_inc(S("max_ready"), 1)
        if part == 2:
            dve.wait_ge(S("probs_ready"), 16 * gp + q + 1)
            nc.vector.reciprocal(small[:, 12 + q % 2:13 + q % 2], small[:, 10 + q % 2:11 + q % 2]
                                 ).then_inc(S("rsum_ready"), 1)
        if part == 5 and i == TT - 1 and j % 2 == 1:
            dve.wait_ge(S("pv_done"), 4 * gp + j + 1)
            if j == 1:
                dve.wait_ge(S("o_stored"), 32 * gp + 1)
            nc.vector.tensor_copy(o_t[:, j // 2, :], b7[:]).then_inc(S("o_ready"), 1)

    def dve_recurrence(dve, s, kt, g):
        tt, k = stage_of(s, kt)
        b = 4 * g + tt
        v4 = lambda bank: bank[:].rearrange("p (h c) -> p h c", h=GH)
        if k == 0 and tt == 0:
            if not (isinstance(g, int) and g == 0):
                dve.wait_ge(S("pv_done"), 4 * g)
            dve.wait_ge(S("c_stored"), 32)
            nc.vector.memset(LM[:], 0.0)
            nc.vector.memset(RM[:], 0.0).then_inc(S("grams_cleared"), 1)
            nc.vector.memset(state[:], 0.0).then_inc(S("state_ready"), 1)
            dve.wait_ge(S("grams_cleared"), g + 1)
        for kk, bank, dst, mask, name in ((1, b4, LM[:, 0], C_STRICT, "LM"), (2, b5, LM[:, 1], C_STRICT, "LM"),
                                          (3, b6, RM[:, 0], C_INCL, "RM"), (4, b7, RM[:, 1], C_INCL, "RM")):
            if k == kk:
                dve.wait_ge(S(name + "_done"), 2 * b + (kk - 1) % 2 + 1)
                if kk == 1 and tt > 0:
                    dve.wait_ge(S("LT_level_ready"), LEVELS * b)
                own_wait(dve, kk)
                nc.vector.copy_predicated(dst.rearrange("p g f c -> p (g f) c"), over_heads(mask).bitcast(U32),
                                          v4(bank)).then_inc(S(name + "_ready"), 1)
        if 6 <= k < 6 + 2 * LEVELS and (k - 6) % 2 == 1:
            m = (k - 6) // 2 + 1
            if m < LEVELS:
                dve.wait_ge(S("dT_done"), (LEVELS - 1) * b + m)
                nc.vector.tensor_tensor(T_inv[:], T_inv[:], v4(b5), ALU.add).then_inc(S("T_ready"), 1)
            dve.wait_ge(S("dTT_done"), LEVELS * b + m)
            nc.vector.tensor_tensor(T_invT[:], T_invT[:], v4(b6), ALU.add).then_inc(S("TT_ready"), 1)
        if k == 20:
            dve.wait_ge(S("Y_done"), b + 1)
            for j in range(GH):
                ins = nc.vector.bn_stats(stats_t[:, j, :], b3[:, j * HD:(j + 1) * HD])
            ins.then_inc(S("y_halves_ready"), 1)
            dve.wait_ge(S("y_halves_ready"), b + 1)
            own_wait(dve, 5)
            for j in range(GH):
                ins = nc.vector.bn_aggr(small[:, 39 + 2 * j:41 + 2 * j], stats_t[:, j, :])
            ins.then_inc(S("y_stats_ready"), 1)
            if tt < TT - 1:
                dve.wait_ge(S("state_step_done"), 3 * g + tt + 1)
                nc.vector.tensor_tensor(state[:], state[:], b4[:, 0:2 * P].rearrange("p (f c) -> p f c", f=2),
                                        ALU.add).then_inc(S("state_sum_ready"), 1)
                dve.wait_ge(S("state_sum_ready"), 3 * g + tt + 1)
                for ft in range(2):
                    ins = nc.vector.scalar_tensor_tensor(out=state[:, ft, :], in0=state[:, ft, :],
                                                         scalar=st_scale[:, ft, tt:tt + 1], in1=const(C_BLK),
                                                         op0=ALU.mult, op1=ALU.mult)
                ins.then_inc(S("state_ready"), 1)
            dve.wait_ge(S("y_rstd_ready"), b + 1)
            for j in range(GH):
                v = slice(j * HD, (j + 1) * HD)
                ins = nc.vector.tensor_scalar(Yn_t[:, v], b3[:, v], small[:, 39 + 2 * j:40 + 2 * j],
                                              small[:, 24 + j:25 + j], ALU.subtract, ALU.mult)
            ins.then_inc(S("y_norm_ready"), 1)

    def pool_arrival_rwkv(pool, s, g):
        n = LORA_SLABS + GROUP_SLABS * g + s - 1
        pool.wait_ge(tile_evacuated, n + 1)
        ft, kind = (s - 1) // 3, (s - 1) % 3
        f = 2 * g + ft
        if kind == 2:
            pool.wait_ge(S("bonus_done"), f + 1)
        if kind == 1:
            pool.wait_ge(S("K_ready"), f + 1)
        nc.gpsimd.tensor_tensor(t1[:], u_t[:, 0:SEQ], u_t[:, 1:SEQ + 1], ALU.subtract).then_inc(S("shift_ready"), 1)

    def pool_rwkv_prep(pool, s, kt, g):
        if s % 3 == 0 and kt == 11:
            pool.wait_ge(S("d_ready"), 2 * g + s // 3 + 1)
            nc.gpsimd.tensor_tensor(sg_t[:], d_t[:], sg_t[:], ALU.subtract).then_inc(S("d_prev_ready"), 1)

    def pool_finish(pool, s, kt, gp):
        if s == 0 and kt in (3, 5):
            ft = (kt - 3) // 2
            pool.wait_ge(S("y_turned_ready"), 4 * gp + 4)
            pool.wait_ge(S("bonus_v_ready"), 2 * gp + ft + 1)
            nc.gpsimd.tensor_tensor(R_t[:, ft, :], R_t[:, ft, :], bonus[:, ft, :], ALU.add
                                    ).then_inc(S("y_plus_bonus"), 1)

    def pool_attention(pool, s, kt, gp):
        q, part = attention_step(s, kt)
        i = q % TT
        if part == 2:
            pool.wait_ge(S("rsum_ready"), 16 * gp + q + 1)
            own_wait(pool, 1 + q % 2)
            nc.gpsimd.tensor_scalar(probs[:, q % 2, 0:(i + 1) * P], probs[:, q % 2, 0:(i + 1) * P],
                                    small[:, 12 + q % 2:13 + q % 2], 1.0, ALU.mult, ALU.mult
                                    ).then_inc(S("probs_normed"), 1)

    def pool_recurrence(pool, s, kt, g):
        tt, k = stage_of(s, kt)
        b = 4 * g + tt
        if k == 2:
            pool.wait_ge(S("LM_ready"), 2 * b + 2)
            if tt > 0:
                pool.wait_ge(S("U_done"), b)
            nc.gpsimd.tensor_tensor(by_parity(T_invT[:]), LM[:, :, 0], by_parity(over_heads(C_LEVEL)), ALU.mult).then_inc(S("pairs_ready"), 1)
            pool.wait_ge(S("pairs_ready"), b + 1)
            nc.gpsimd.tensor_tensor(T_invT[:], T_invT[:], over_heads(C_ID), ALU.add).then_inc(S("TT0_ready"), 1)
        if 2 <= k < 2 + 2 * LEVELS and k % 2 == 0:
            m = k // 2
            if m > 2:
                pool.wait_ge(S("X_done"), LEVELS * b + m - 2)
            nc.gpsimd.tensor_tensor(by_parity(LTm[:, (m - 1) % 2]), LM[:, :, 0],
                                    by_parity(over_heads(C_LEVEL + m * P)), ALU.mult
                                    ).then_inc(S("LT_level_ready"), 1)


    def dve_arrival_lora(dve, m):
        if m == 0:
            dve.wait_ge(S("norm_ready"), NORM_X)
        if m == 2:
            dve.wait_ge(S("xa_ready"), 1)
        if m == 3:
            dve.wait_ge(S("lora_mixed"), 2)
        evacuate(dve, m, m % 2).then_inc(tile_evacuated, 1)
        dve.wait_ge(S("shift_ready"), m + 1)
        if m == 2:
            dve.wait_ge(S("tanh_ready"), 1)
        if m == 3:
            dve.wait_ge(S("sig_g_ready"), 1)
        dst = xa_t if m == 1 else t2
        nc.vector.scalar_tensor_tensor(out=dst[:], in0=t1[:], scalar=gain_of("mu")[:, m:m + 1],
                                       in1=u_t[:, 1:SEQ + 1], op0=ALU.mult, op1=ALU.add
                                       ).then_inc(S("xa_ready") if m == 1 else S("lora_mixed"), 1)
        if m == 0:
            fs = slice(LORA, LORA + 16)
            dve.wait_ge(S("lora_mixed"), 1)
            nc.vector.tensor_scalar(cf[fs, 0, :], t2[fs, :], gain_of("f_bias")[fs, :], None, ALU.add
                                    ).then_inc(S("forget_step"), 1)
            dve.wait_ge(S("forget_step"), 1)
            nc.vector.scalar_tensor_tensor(out=cf[fs, 1, :], in0=cf[fs, 0, :], scalar=-1.0, in1=cf[fs, 0, :],
                                           op0=ALU.mult, op1=ALU.max).then_inc(S("forget_step"), 1)
            dve.wait_ge(S("forget_log_step"), 2)
            nc.vector.scalar_tensor_tensor(out=cf[fs, 1, :], in0=cf[fs, 0, :], scalar=0.0, in1=cf[fs, 1, :],
                                           op0=ALU.min, op1=ALU.subtract).then_inc(S("forget_step"), 1)
            dve.wait_ge(S("forget_step"), 3)
            for tt in range(TT):
                if tt:
                    dve.wait_ge(S("forget_step"), 3 + tt)
                nc.vector.tensor_tensor_scan(cf[fs, 0, tok(tt)], ones[fs, :], cf[fs, 1, tok(tt)],
                                             cf[fs, 0, tt * P - 1:tt * P] if tt else 0.0, ALU.mult, ALU.add
                                             ).then_inc(S("forget_step"), 1)
            dve.wait_ge(S("forget_step"), 3 + TT)
            nc.vector.tensor_scalar(cf[fs, 1, :], cf[fs, 0, :], -1.0, None, ALU.mult).then_inc(S("c_ready"), 1)

    def act_arrival_lora(act, m):
        if m == 0:
            act.wait_ge(S("lora_mixed"), 1)
            nc.scalar.activation(tanh_w[0:LORA, :], t2[0:LORA, :], ACT.Tanh).then_inc(S("tanh_ready"), 1)
            fs = slice(LORA, LORA + 16)
            act.wait_ge(S("forget_step"), 2)
            nc.scalar.activation(cf[fs, 1, :], cf[fs, 1, :], ACT.Exp, scale=-1.0).then_inc(S("forget_log_step"), 1)
            act.wait_ge(S("forget_log_step"), 1)
            nc.scalar.activation(cf[fs, 1, :], cf[fs, 1, :], ACT.Ln, bias=1.0).then_inc(S("forget_log_step"), 1)
        if m >= 2:
            act.wait_ge(S("lora_mixed"), m)
            nc.scalar.activation(sig_g[:, m - 2, :], t2[:], ACT.Sigmoid).then_inc(S("sig_g_ready"), 1)

    def pool_arrival_lora(pool, m):
        pool.wait_ge(tile_evacuated, m + 1)
        nc.gpsimd.tensor_tensor(t1[:], u_t[:, 0:SEQ], u_t[:, 1:SEQ + 1], ALU.subtract).then_inc(S("shift_ready"), 1)

    def hn_steps(gain):
        def on_act(act, o, tile, idx, norm):
            act.wait_ge(tile_evacuated, tile + 1)
            nc.scalar.activation(hn_hi[:, o, :], h_t[:, o, :], ACT.Copy, scale=gain_of(gain)[:, o_col(o)]
                                 ).then_inc(S("hn_hi_ready"), 1)
            act.wait_ge(S("h_summed"), idx + norm)
            own_wait(act)
            nc.scalar.activation(sq_s[:], h_t[:, o, :], ACT.Square).then_inc(S("h_squared"), 1)

        def on_dve(dve, o, idx):
            dve.wait_ge(S("hn_hi_ready"), idx + 1)
            nc.vector.scalar_tensor_tensor(out=hn_lo[:, o, :], in0=h_t[:, o, :], scalar=gain_of(gain)[:, o_col(o)],
                                           in1=hn_hi[:, o, :].bitcast(F32), op0=ALU.mult, op1=ALU.subtract
                                           ).then_inc(S("hn_ready"), 1)

        def on_pool(pool, idx):
            pool.wait_ge(S("h_squared"), idx + 1)
            nc.gpsimd.tensor_tensor(acc_h[:], acc_h[:], sq_s[:], ALU.add).then_inc(S("h_summed"), 1)
        return on_act, on_dve, on_pool

    def o_col(o):
        return slice(o, o + 1) if isinstance(o, int) else bass.ds(o, 1)

    ffn_norm, gate_norm = hn_steps("ffn_g"), hn_steps("gate_g")
    gate_slab_cols = (HALF * P, HALF * P)
    down_cols = tuple(k * P for k in DOWN_HALVES)

    def pairs(eng, count, body):
        with eng.Fori(0, count - 1) as i:
            body(i, False)
        body(count - 1, True)

    def group_loop(eng, group):
        group(0, None)
        with eng.Fori(0, GROUPS - 1) as i:
            group(i + 1, i)

    slab_of = lambda g, s: LORA_SLABS + GROUP_SLABS * g + s
    ffn_base = lambda c: N_FFN + CHUNK_SLABS * c
    down_base = lambda c: N_FFN + CHUNK_SLABS * c + 2 * CF

    with nc.Block() as block:

        @block.sync
        def _(sp):
            load_slab(sp, 0, d["w_mix"][0])
            sp.dma_start(par[:], d["params"]).then_inc(S("par_landed"), 16)
            sp.dma_start(consts[:], d["consts"]).then_inc(S("consts_landed"), 16)
            sp.dma_start(ones[:], d["consts"][:, C_ONE:C_ONE + P]).then_inc(S("ones_landed"), 16)
            sp.dma_start(ccol[:], d["consts"][:, C_COL:C_COL + 8]).then_inc(S("ones_landed"), 16)
            sp.dma_start(id16[:], d["id16"]).then_inc(S("consts_landed"), 16)
            x_quarter = lambda i: d["xT"][4 * i:4 * i + 4].rearrange("k p t -> p k t")
            for i in range(4):
                sp.dma_start(x_raw[:, 4 * i:4 * i + 4, :], x_quarter(i)).then_inc(S(f"input_landed_{i}"), 16)
            load_slab(sp, 1, d["w_mix"][1])

            def group_loads(g):
                sp.dma_start(g_par[:], d["g_params"][g]).then_inc(S("g_par_landed"), 16)
                for i, w in enumerate(("w2", "a2")):
                    sp.dma_start(w2a2[0:LORA, i, :], d[w][g]).then_inc(S("g_weights_landed"), 16)

            sp.wait_ge(S("in_ready"), KT)
            sp.wait_ge(S("x_summed_pool"), KT // 2)
            sp.wait_ge(S("x_summed_dve"), KT // 2)
            group_loads(0)
            for n in range(LORA_SLABS):
                load_slab(sp, n + 2, d["w_mix"][n + 2])
                if n == 1:
                    sp.wait_ge(S("c_ready"), 1)
                    for i in range(2):
                        sp.dma_start(c_dram[i], cf[LORA:LORA + 16, i, :]).then_inc(S("c_stored"), 16)

            def store_rwkv(gp):
                sp.wait_ge(S("y_rwkv_ready"), 2 * gp + 2)
                for ft in range(2):
                    sp.dma_start(y_dram[2 * gp + ft], R_t[:, ft, :]).then_inc(S("y_rwkv_stored"), 16)

            def store_fox(gp):
                sp.wait_ge(S("o_ready"), 2 * gp + 2)
                for pr in range(2):
                    sp.dma_start(y_dram[2 * GROUPS + 2 * gp + pr], o_t[:, pr, :]).then_inc(S("o_stored"), 16)

            def group(g, gp):
                for s in range(GROUP_SLABS):
                    load_slab(sp, slab_of(g, s) + 2, d["w_mix"][slab_of(g, s) + 2])
                    if gp is not None:
                        if s == 0:
                            sp.wait_ge(S("y_turned_ready"), 4 * g)
                            group_loads(g)
                        if s == 1:
                            store_rwkv(gp)
                        if s == 6:
                            store_fox(gp)
                    if s == 6:
                        sp.dma_start(g2_t[:], d["g2"][g]).then_inc(S("g2_landed"), 16)
                        sp.wait_ge(S("c_stored"), 32)
                        sp.wait_ge(S("aug_ones_ready"), 2)
                        cg = bass.ds(GH * g, GH) if gp is not None else slice(0, GH)
                        sp.dma_start(q_aug[HD + 1:HD + 2, :, :], c_dram[0:1, cg, :]).then_inc(S("c_rows_landed"), 16)
                        sp.dma_start(k_aug[HD:HD + 1, :, :], c_dram[1:2, cg, :]).then_inc(S("c_rows_landed"), 16)

            group_loop(sp, group)
            store_rwkv(GROUPS - 1)
            store_fox(GROUPS - 1)
            sp.wait_ge(S("y_rwkv_stored"), 32 * GROUPS)
            sp.wait_ge(S("o_stored"), 32 * GROUPS + 1)
            for i in range(4):
                sp.dma_start(h_t[:, 4 * i:4 * i + 4, :], y_dram[4 * i:4 * i + 4].rearrange("k p t -> p k t")
                             ).then_inc(S(f"input_landed_{i}"), 16)
            for i in range(4):
                sp.wait_ge(S("in_ready"), KT + 4 * i + 4)
                sp.dma_start(h_t[:, 4 * i:4 * i + 4, :], x_quarter(i)).then_inc(S(f"input_landed_{i}"), 16)
            with sp.Fori(0, OUT_SLABS - 2) as o:
                load_slab(sp, N_OUT + 2 + o, d["w_mix"][N_OUT + 2 + o])
            with sp.Fori(0, 2) as i:
                load_slab(sp, N_FFN + i, d["w_gu"][i])
            sp.wait_ge(weights_used, 2 * N_FFN)
            sp.dma_start(p_raw[:], d["pT"]).then_inc(S("p_landed"), 16)
            with sp.Fori(2, 2 * CF) as i:
                load_slab(sp, N_FFN + i, d["w_gu"][i])
            with sp.Fori(0, OUT_SLABS) as o:
                load_slab(sp, down_base(0) + o, d["w_down"][o], down_cols)
            with sp.Fori(1, CHUNKS) as c:
                with sp.Fori(0, 2 * CF) as i:
                    load_slab(sp, ffn_base(c) + i, d["w_gu"][2 * CF * c + i])
                with sp.Fori(0, OUT_SLABS) as o:
                    load_slab(sp, down_base(c) + o, d["w_down"][OUT_SLABS * c + o], down_cols)
            for u in range(PROJ_SLABS):
                load_slab(sp, N_PROJ + u, d["ple_proj"][u])
            with sp.Fori(0, OUT_SLABS) as o:
                load_slab(sp, N_GATE + o, d["ple_gate"][o])

        @block.tensor
        def _(pe):
            pe.wait_ge(S("consts_landed"), 32)
            pe.wait_ge(S("ones_landed"), 32)
            for n in range(LORA_SLABS):
                multiply_slab(pe, n, n % 2, in_hi, in_lo,
                              input_ready=(lambda kt: pe.wait_ge(S("in_ready"), kt + 1)) if n == 0 else None)
                if n == 0:
                    pe.wait_ge(S("x_summed_dve"), KT // 2)
                    pe.wait_ge(S("x_summed_pool"), KT // 2)
                    for i in range(2):
                        last = nc.tensor.matmul(aux[:], ones[:], acc_x[:, i, :], start=i == 0, stop=i == 1,
                                                skip_group_check=True)
                    last.then_inc(S("norm_summed"), 1)

            def group(g, gp):
                for s in range(GROUP_SLABS):
                    def side(kt):
                        if s < 6:
                            if gp is not None:
                                pe_attention(pe, s, kt, gp)
                                pe_finish(pe, s, kt, gp)
                            pe_rwkv_prep(pe, s, kt, g)
                        else:
                            pe_fox_prep(pe, s, kt, g)
                            pe_recurrence(pe, s, kt, g)
                    multiply_slab(pe, slab_of(g, s), s % 2, in_hi, in_lo, side=side)

            group_loop(pe, group)
            for s in range(6):
                for kt in range(KT):
                    pe_attention(pe, s, kt, GROUPS - 1)
                    pe_finish(pe, s, kt, GROUPS - 1)

            out_slab_waits = lambda kt: pe.wait_ge(S("in_ready"), KT + kt + 1)
            for j in range(2):
                multiply_slab(pe, N_OUT + j, j, in_hi, in_lo, input_ready=out_slab_waits if j == 0 else None)
            with pe.Fori(1, OUT_SLABS // 2) as i:
                for j in range(2):
                    multiply_slab(pe, N_OUT + 2 * i + j, j, in_hi, in_lo)

            def gate_up_pair(c, i, first):
                for j in range(2):
                    def side(kt):
                        if first and j == 0:
                            pe.wait_ge(S("hn_ready"), kt + 1)
                        if first and j == 0 and kt == 15:
                            pe.wait_ge(S("h_summed"), KT + 1)
                            nc.tensor.matmul(aux[:], ones[:], acc_h[:], start=True, stop=True,
                                             skip_group_check=True).then_inc(S("norm_summed"), 1)
                    multiply_slab(pe, ffn_base(c) + 2 * i + j, j, hn_hi, hn_lo, side=side)

            def down(c):
                with pe.Fori(0, OUT_SLABS // 2) as i:
                    for j in range(2):
                        def side(kt):
                            if j == 0 and kt == 0:
                                pe.wait_ge(S("low_part_ready"), 2 + CF * c + DOWN_HALVES[0])
                            if j == 0 and kt == DOWN_HALVES[0]:
                                pe.wait_ge(S("low_part_ready"), 2 + CF * c + CF)
                        multiply_slab(pe, down_base(c) + 2 * i + j, j, act_hi, act_lo, kts=DOWN_HALVES, side=side)

            gate_up_pair(0, 0, True)
            with pe.Fori(1, CF) as i:
                gate_up_pair(0, i, False)
            down(0)
            with pe.Fori(1, CHUNKS) as c:
                with pe.Fori(0, CF) as i:
                    gate_up_pair(c, i, False)
                down(c)
            pe.wait_ge(S("low_part_ready"), 2)
            for u in range(PROJ_SLABS):
                for r in range(PROJ_TILES):
                    tile = N_PROJ + PROJ_TILES * u + r
                    pe.wait_ge(tile_evacuated, tile - 1)
                    if r % 4 == 0:
                        pe.wait_ge(lo_ready, 2 * (N_PROJ + u) + r // 4 + 1)
                    for k in range(2):
                        last = three_products(psum[tile % 2][:], ring_slots(u % 2, r // 4), ((r % 4) * 2 + k) * P,
                                              p_hi[:, k, :], p_lo[:, k, :], k == 0, k == 1)
                    last.then_inc(weights_used if r % 4 == 3 else S("proj_done"), 1)
                if u == 0:
                    pe.wait_ge(S("h_summed"), 2 * KT + 2)
                    pe.wait_ge(S("norm_ready"), NORM_FFN)
                    nc.tensor.matmul(aux[:], ones[:], acc_h[:], start=True, stop=True).then_inc(S("norm_summed"), 1)

            def gate_slab(o, j, first):
                def side(kt):
                    if first and kt == 15:
                        pe.wait_ge(S("e_summed"), KT)
                        pe.wait_ge(S("norm_ready"), NORM_GATE)
                        nc.tensor.matmul(aux[:], ones[:], acc_e[:], start=True, stop=True,
                                         skip_group_check=True).then_inc(S("norm_summed"), 1)
                after(pe, tile_evacuated, TILE_GATE + o - 1)
                multiply_slab(pe, N_GATE + o, j, hn_hi, hn_lo, side=side)

            pe.wait_ge(S("hn_ready"), 2 * KT)
            gate_slab(0, 0, True)
            gate_slab(1, 1, False)
            with pe.Fori(1, OUT_SLABS // 2) as i:
                for j in range(2):
                    gate_slab(2 * i + j, j, False)

        @block.scalar
        def _(act):
            act.wait_ge(S("par_landed"), 16)
            nc.scalar.activation(scratch[mybir.EngineType.Activation][:, 0:2], par[:, 0:2], ACT.Copy)
            round_slab(act, 0, 0)
            for kt in range(KT):
                act.wait_ge(S(f"input_landed_{kt // 4}"), 16)
                nc.scalar.activation(in_hi[:, kt, :], x_raw[:, kt, :], ACT.Copy, scale=gain_of("attn_g")[:, kt:kt + 1]
                                     ).then_inc(S("in_hi_ready"), 1)
            for kt in range(KT):
                if kt >= 2:
                    act.wait_ge(S("x_summed_dve" if kt % 2 == 0 else "x_summed_pool"), kt // 2)
                nc.scalar.activation(sqx[:, kt % 2, :], x_raw[:, kt, :], ACT.Square
                                     ).then_inc(S("x_squared_even" if kt % 2 == 0 else "x_squared_odd"), 1)
            round_slab(act, 1, 1)

            def rstd(dst, norm):
                act.wait_ge(S("norm_summed"), norm)
                nc.scalar.activation(dst[:], aux[:], ACT.Ln, scale=1.0 / D_MODEL, bias=cb(CB_RMS)
                                     ).then_inc(S("norm_logged"), 1)
                act.wait_ge(S("norm_logged"), norm)
                nc.scalar.activation(dst[:], dst[:], ACT.Exp, scale=-0.5).then_inc(S("norm_ready"), 1)

            act.wait_ge(S("ones_landed"), 32)
            rstd(rstd_x, NORM_X)
            for n in range(1, LORA_SLABS):
                act_arrival_lora(act, n - 1)
                round_slab(act, n + 1, (n + 1) % 2)

            def group(g, gp):
                for s in range(GROUP_SLABS):
                    if s == 0 and gp is None:
                        act_arrival_lora(act, LORA_SLABS - 1)
                    round_slab(act, slab_of(g, s) + 1, (s + 1) % 2)
                    for kt in range(KT):
                        if s < 6:
                            if gp is not None:
                                act_attention(act, s, kt, gp)
                                act_finish(act, s, kt, gp)
                            act_rwkv_prep(act, s, kt, g)
                        else:
                            act_fox_prep(act, s, kt, g)
                            act_recurrence(act, s, kt, g)

            group_loop(act, group)
            for s in range(6):
                for kt in range(KT):
                    act_attention(act, s, kt, GROUPS - 1)
                    act_finish(act, s, kt, GROUPS - 1)
            for kt in range(KT):
                act.wait_ge(S(f"input_landed_{kt // 4}"), 32)
                nc.scalar.activation(in_hi[:, kt, :], h_t[:, kt, :], ACT.Copy).then_inc(S("in_hi_ready"), 1)

            def out_pair(i, last):
                for j in range(2):
                    n = N_OUT + 2 * i + j
                    round_slab(act, n + 1, (j + 1) % 2)
                    ffn_norm[0](act, 2 * i + j, n, 2 * i + j, 1)
            pairs(act, OUT_SLABS // 2, out_pair)
            rstd(rstd_h, NORM_FFN)

            def gate_up_pair(c, i, last):
                for j in range(2):
                    n = ffn_base(c) + 2 * i + j
                    round_slab(act, n + 1, (j + 1) % 2, down_cols if last and j == 1 else gate_slab_cols)
                    t = CF * c + i
                    if j == 0:
                        act.wait_ge(tile_evacuated, n + 1)
                        nc.scalar.activation(silu_s[:], gate_s[:], ACT.Silu).then_inc(S("silu_ready"), 1)
                    else:
                        act.wait_ge(S("act_product_ready"), t + 1)
                        nc.scalar.activation(act_hi[:, i, :], up_s[:], ACT.Copy).then_inc(S("act_hi_ready"), 1)

            def down_pair(c, i, last, final):
                for j in range(2):
                    n = down_base(c) + 2 * i + j
                    whole = last and j == 1
                    round_slab(act, n + 1, (j + 1) % 2, gate_slab_cols if whole else down_cols)
                    if final:
                        gate_norm[0](act, 2 * i + j, n, KT + 2 * i + j, 2)

            act.wait_ge(S("p_landed"), 16)
            for k in range(2):
                nc.scalar.activation(p_hi[:, k, :], p_raw[:, k, :], ACT.Copy).then_inc(S("p_hi_ready"), 1)
            with act.Fori(0, CHUNKS - 1) as c:
                pairs(act, CF, lambda i, last: gate_up_pair(c, i, last))
                pairs(act, OUT_SLABS // 2, lambda i, last: down_pair(c, i, last, False))
            pairs(act, CF, lambda i, last: gate_up_pair(CHUNKS - 1, i, last))
            pairs(act, OUT_SLABS // 2, lambda i, last: down_pair(CHUNKS - 1, i, last, True))
            for u in range(PROJ_SLABS):
                round_slab(act, N_PROJ + u + 1, (u + 1) % 2)
                for r in range(PROJ_TILES):
                    t = PROJ_TILES * u + r
                    act.wait_ge(tile_evacuated, N_PROJ + t + 1)
                    act.wait_ge(S("h_summed"), 2 * KT + 2)
                    after(act, S("e_summed"), t)
                    nc.scalar.activation(sq_s[:], e_t[:, t, :], ACT.Square).then_inc(S("e_squared"), 1)
                if u == 0:
                    rstd(rstd_h, NORM_GATE)

            def gate_slot(o, j, last):
                if not last:
                    round_slab(act, N_GATE + o + 1, (j + 1) % 2)
                if isinstance(o, int) and o == 0:
                    rstd(rstd_e, NORM_E)
                act.wait_ge(tile_evacuated, TILE_GATE + o + 1)
                nc.scalar.activation(silu_s[:], gate_s[:], ACT.Sigmoid, bias=gain_of("gate_b")[:, o_col(o)]
                                     ).then_inc(S("gate_ready"), 1)

            gate_slot(0, 0, False)
            gate_slot(1, 1, False)
            with act.Fori(1, OUT_SLABS // 2 - 1) as i:
                for j in range(2):
                    gate_slot(2 * i + j, j, False)
            gate_slot(OUT_SLABS - 2, 0, False)
            gate_slot(OUT_SLABS - 1, 1, True)

        @block.vector
        def _(dve):
            dve.wait_ge(S("par_landed"), 16)
            subtract_slab(dve, 0, 0)
            for kt in range(KT):
                dve.wait_ge(S("in_hi_ready"), kt + 1)
                nc.vector.scalar_tensor_tensor(out=in_lo[:, kt, :], in0=x_raw[:, kt, :],
                                               scalar=gain_of("attn_g")[:, kt:kt + 1],
                                               in1=in_hi[:, kt, :].bitcast(F32), op0=ALU.mult, op1=ALU.subtract
                                               ).then_inc(S("in_ready"), 1)
            nc.vector.memset(scratch[mybir.EngineType.DVE][:, 0:1], 0.0).then_inc(S("o_stored"), 1)
            nc.vector.memset(acc_x[:, 0, :], 0.0).then_inc(S("acc_cleared"), 1)
            dve.wait_ge(S("acc_cleared"), 1)
            for i in range(KT // 2):
                dve.wait_ge(S("x_squared_even"), i + 1)
                after(dve, S("x_summed_dve"), i)
                nc.vector.tensor_tensor(acc_x[:, 0, :], acc_x[:, 0, :], sqx[:, 0, :], ALU.add
                                        ).then_inc(S("x_summed_dve"), 1)
            nc.vector.tensor_scalar(qg8[:], gain_of("q_g"), HD ** -0.5, None, ALU.mult).then_inc(S("q_gain_ready"), 1)
            subtract_slab(dve, 1, 1)
            dve.wait_ge(S("ones_landed"), 32)
            dve.wait_ge(S("consts_landed"), 32)
            dve.wait_ge(S("q_gain_ready"), 1)
            dve.wait_ge(S("aug_ones_ready"), 2)
            dve.wait_ge(S("u_column_cleared"), 1)
            for n in range(1, LORA_SLABS):
                dve_arrival_lora(dve, n - 1)
                subtract_slab(dve, n + 1, (n + 1) % 2)

            def group(g, gp):
                for s in range(GROUP_SLABS):
                    if s == 0:
                        if gp is None:
                            dve_arrival_lora(dve, LORA_SLABS - 1)
                        else:
                            dve_arrival_fox(dve, GROUP_SLABS, gp)
                    elif s <= 6:
                        dve_arrival_rwkv(dve, s, g)
                    else:
                        dve_arrival_fox(dve, s, g)
                    subtract_slab(dve, slab_of(g, s) + 1, (s + 1) % 2)
                    for kt in range(KT):
                        if s < 6:
                            if gp is not None:
                                dve_attention(dve, s, kt, gp)
                                dve_finish(dve, s, kt, gp)
                            dve_rwkv_prep(dve, s, kt, g)
                        else:
                            dve_fox_prep(dve, s, kt, g)
                            dve_recurrence(dve, s, kt, g)

            group_loop(dve, group)
            dve_arrival_fox(dve, GROUP_SLABS, GROUPS - 1)
            for s in range(6):
                for kt in range(KT):
                    dve_attention(dve, s, kt, GROUPS - 1)
                    dve_finish(dve, s, kt, GROUPS - 1)
            for kt in range(KT):
                dve.wait_ge(S("in_hi_ready"), KT + kt + 1)
                nc.vector.tensor_tensor(in_lo[:, kt, :], h_t[:, kt, :], in_hi[:, kt, :].bitcast(F32), ALU.subtract
                                        ).then_inc(S("in_ready"), 1)

            def add_to_residual(o, n, j):
                dve.wait_ge(weights_used, 2 * n + 2)
                nc.vector.tensor_tensor(h_t[:, o, :], h_t[:, o, :], psum[j][:], ALU.add).then_inc(tile_evacuated, 1)

            for i in range(4):
                dve.wait_ge(S(f"input_landed_{i}"), 48)

            def out_pair(i, last):
                for j in range(2):
                    o, n = 2 * i + j, N_OUT + 2 * i + j
                    subtract_slab(dve, n + 1, (j + 1) % 2)
                    add_to_residual(o, n, j)
                    ffn_norm[1](dve, o, o)
            pairs(dve, OUT_SLABS // 2, out_pair)
            dve.wait_ge(S("norm_ready"), NORM_FFN)

            def gate_up_pair(c, i, last):
                for j in range(2):
                    n = ffn_base(c) + 2 * i + j
                    subtract_slab(dve, n + 1, (j + 1) % 2, down_cols if last and j == 1 else gate_slab_cols)
                    t = CF * c + i
                    dve.wait_ge(weights_used, 2 * n + 2)
                    if j == 0:
                        nc.vector.tensor_tensor(gate_s[:], psum[0][:], rstd_h[:], ALU.mult
                                                ).then_inc(tile_evacuated, 1)
                    else:
                        dve.wait_ge(S("low_part_ready"), 2 + t)
                        nc.vector.tensor_tensor(up_s[:], psum[1][:], rstd_h[:], ALU.mult
                                                ).then_inc(tile_evacuated, 1)
                        dve.wait_ge(tile_evacuated, n + 1)
                        dve.wait_ge(S("silu_ready"), t + 1)
                        nc.vector.tensor_tensor(up_s[:], up_s[:], silu_s[:], ALU.mult
                                                ).then_inc(S("act_product_ready"), 1)
                        dve.wait_ge(S("act_hi_ready"), t + 1)
                        nc.vector.tensor_tensor(act_lo[:, i, :], up_s[:], act_hi[:, i, :].bitcast(F32), ALU.subtract
                                                ).then_inc(S("low_part_ready"), 1)

            def down_pair(c, i, last, final):
                for j in range(2):
                    o, n = 2 * i + j, down_base(c) + 2 * i + j
                    subtract_slab(dve, n + 1, (j + 1) % 2, gate_slab_cols if last and j == 1 else down_cols)
                    add_to_residual(o, n, j)
                    if final:
                        gate_norm[1](dve, o, KT + o)

            for k in range(2):
                dve.wait_ge(S("p_hi_ready"), k + 1)
                nc.vector.tensor_tensor(p_lo[:, k, :], p_raw[:, k, :], p_hi[:, k, :].bitcast(F32), ALU.subtract
                                        ).then_inc(S("low_part_ready"), 1)
            with dve.Fori(0, CHUNKS - 1) as c:
                pairs(dve, CF, lambda i, last: gate_up_pair(c, i, last))
                pairs(dve, OUT_SLABS // 2, lambda i, last: down_pair(c, i, last, False))
            pairs(dve, CF, lambda i, last: gate_up_pair(CHUNKS - 1, i, last))
            pairs(dve, OUT_SLABS // 2, lambda i, last: down_pair(CHUNKS - 1, i, last, True))
            for u in range(PROJ_SLABS):
                subtract_slab(dve, N_PROJ + u + 1, (u + 1) % 2)
                for r in range(PROJ_TILES):
                    t = PROJ_TILES * u + r
                    if r % 4 == 3:
                        dve.wait_ge(weights_used, 2 * (N_PROJ + u) + r // 4 + 1)
                    else:
                        dve.wait_ge(S("proj_done"), 3 * (t // 4) + t % 4 + 1)
                    nc.vector.tensor_copy(e_t[:, t, :], psum[(N_PROJ + t) % 2][:]).then_inc(tile_evacuated, 1)

            def gate_slot(o, j, last):
                n = N_GATE + o
                if not last:
                    subtract_slab(dve, n + 1, (j + 1) % 2)
                if isinstance(o, int) and o == 0:
                    dve.wait_ge(S("norm_ready"), NORM_GATE)
                    dve.wait_ge(S("norm_ready"), NORM_E)
                if not (isinstance(o, int) and o == 0):
                    dve.wait_ge(S("out_ready"), o)
                nc.vector.scalar_tensor_tensor(out=up_s[:], in0=e_t[:, o, :], scalar=gain_of("ple_g")[:, o_col(o)],
                                               in1=rstd_e[:], op0=ALU.mult, op1=ALU.mult).then_inc(S("e_ready"), 1)
                dve.wait_ge(weights_used, 2 * n + 2)
                nc.vector.tensor_tensor(gate_s[:], psum[j][:], rstd_h[:], ALU.mult
                                        ).then_inc(tile_evacuated, 1)
                dve.wait_ge(S("gate_ready"), o + 1)
                dve.wait_ge(S("e_ready"), o + 1)
                nc.vector.tensor_tensor(up_s[:], up_s[:], silu_s[:], ALU.mult).then_inc(S("gated"), 1)
                dve.wait_ge(S("gated"), o + 1)
                nc.vector.tensor_tensor(h_t[:, o, :], h_t[:, o, :], up_s[:], ALU.add).then_inc(S("out_ready"), 1)

            gate_slot(0, 0, False)
            gate_slot(1, 1, False)
            with dve.Fori(1, OUT_SLABS // 2 - 1) as i:
                for j in range(2):
                    gate_slot(2 * i + j, j, False)
            gate_slot(OUT_SLABS - 2, 0, False)
            gate_slot(OUT_SLABS - 1, 1, True)

        @block.gpsimd
        def _(pool):
            nc.gpsimd.memset(scratch[mybir.EngineType.Pool][:], 0.0)
            nc.gpsimd.memset(acc_x[:, 1, :], 0.0).then_inc(S("sums_cleared"), 1)
            pool.wait_ge(S("sums_cleared"), 1)
            for i in range(KT // 2):
                pool.wait_ge(S("x_squared_odd"), i + 1)
                after(pool, S("x_summed_pool"), i)
                nc.gpsimd.tensor_tensor(acc_x[:, 1, :], acc_x[:, 1, :], sqx[:, 1, :], ALU.add
                                        ).then_inc(S("x_summed_pool"), 1)
            pool.wait_ge(S("in_ready"), KT)
            pool.wait_ge(S("x_summed_dve"), KT // 2)
            pool.wait_ge(S("x_summed_pool"), KT // 2)
            nc.gpsimd.memset(u_t[:, 0:1], 0.0).then_inc(S("u_column_cleared"), 1)
            pool.wait_ge(S("u_column_cleared"), 1)
            for i, t in enumerate((q_aug, k_aug)):
                after(pool, S("aug_ones_ready"), i)
                nc.gpsimd.memset(t[HD:HD + 2, :, :], 1.0).then_inc(S("aug_ones_ready"), 1)
            pool.wait_ge(S("aug_ones_ready"), 2)
            pool.wait_ge(S("consts_landed"), 32)
            for n in range(1, LORA_SLABS):
                pool_arrival_lora(pool, n - 1)

            def group(g, gp):
                for s in range(GROUP_SLABS):
                    if s == 0:
                        if gp is None:
                            pool_arrival_lora(pool, LORA_SLABS - 1)
                    elif s <= 6:
                        pool_arrival_rwkv(pool, s, g)
                    for kt in range(KT):
                        if s < 6:
                            if gp is not None:
                                pool_attention(pool, s, kt, gp)
                                pool_finish(pool, s, kt, gp)
                            pool_rwkv_prep(pool, s, kt, g)
                        else:
                            pool_recurrence(pool, s, kt, g)

            group_loop(pool, group)
            for s in range(6):
                for kt in range(KT):
                    pool_attention(pool, s, kt, GROUPS - 1)
                    pool_finish(pool, s, kt, GROUPS - 1)
            pool.wait_ge(S("y_rwkv_stored"), 32 * GROUPS)
            pool.wait_ge(S("o_stored"), 32 * GROUPS + 1)
            nc.gpsimd.memset(acc_h[:], 0.0).then_inc(S("h_summed"), 1)

            def sum_squares(first):
                with pool.Fori(0, KT) as o:
                    ffn_norm[2](pool, first + o)
            sum_squares(0)
            pool.wait_ge(S("norm_summed"), NORM_FFN)
            nc.gpsimd.memset(acc_h[:], 0.0).then_inc(S("h_summed"), 1)
            sum_squares(KT)
            pool.wait_ge(weights_used, 2 * N_PROJ)
            nc.gpsimd.memset(acc_e[:], 0.0).then_inc(S("sums_cleared"), 1)
            pool.wait_ge(S("sums_cleared"), 2)
            with pool.Fori(0, KT) as o:
                pool.wait_ge(S("e_squared"), o + 1)
                nc.gpsimd.tensor_tensor(acc_e[:], acc_e[:], sq_s[:], ALU.add).then_inc(S("e_summed"), 1)
            with pool.Fori(0, OUT_SLABS) as o:
                pool.wait_ge(S("out_ready"), o + 1)
                pool.dma_start(d["out"][o], h_t[:, o, :]).then_inc(S("out_stored"), 16)
            pool.wait_ge(S("out_stored"), 16 * OUT_SLABS)


def tiles(w):
    k, n = w.shape
    return w.reshape(k // P, P, n // P, P).transpose(2, 1, 0, 3).reshape(n // P, P, k)


def columns(v):
    return v.reshape(-1, P).T


def kernel(x, p, attn_norm_g, w_in, shift_mu, w0, w2, a0, a2, g2, k_k, k_a, r_k, lnx_g, lnx_b, q_norm_g,
           k_norm_g, fgate_b, w_out, ffn_norm_g, w_gate, w_up, w_down, ple_proj, ple_norm_g, ple_gate_norm_g,
           ple_gate_w, ple_gate_b):
    import numpy as np
    import concourse.bacc as bacc
    from concourse.bass_utils import run_bass_kernel_spmd

    A = lambda v: np.asarray(v)[0]
    wi, mu = A(w_in), A(shift_mu)
    RW = 1024
    lora0 = 3 * RW
    fox0 = lora0 + 2 * LORA + 2 * P
    f0 = fox0 + 3 * RW
    z = lambda *s: np.zeros(s, np.float32)
    parts = [wi[:, lora0:lora0 + LORA], wi[:, f0:f0 + 16], z(D_MODEL, P - LORA - 16),
             wi[:, lora0 + LORA:lora0 + 2 * LORA], z(D_MODEL, P - LORA), wi[:, lora0 + 2 * LORA:fox0]]
    for g in range(GROUPS):
        for ft in range(2):
            c = P * (2 * g + ft)
            parts += [wi[:, RW + c:RW + c + P], wi[:, c:c + P], wi[:, 2 * RW + c:2 * RW + c + P]]
        for kind in range(3):
            c = fox0 + RW * kind + 2 * P * g
            parts.append(wi[:, c:c + 2 * P])
    w_mix = np.concatenate([tiles(np.concatenate(parts, 1)), tiles(A(w_out))])
    gu = np.stack([tiles(A(w_gate)), tiles(A(w_up))], 1).reshape(2 * D_FF // P, P, D_MODEL)
    down = np.concatenate([tiles(A(w_down)[c * CF * P:(c + 1) * CF * P]) for c in range(CHUNKS)])
    proj = tiles(A(ple_proj)).reshape(PROJ_SLABS, PROJ_TILES, P, 2 * P).transpose(0, 2, 1, 3).reshape(
        PROJ_SLABS, P, D_MODEL)

    par = z(P, N_PAR)
    put = lambda name, v: par.__setitem__((slice(None), slice(PAR[name][0], PAR[name][0] + v.shape[1])), v)
    for name, v in (("attn_g", attn_norm_g), ("ffn_g", ffn_norm_g), ("gate_g", ple_gate_norm_g),
                    ("ple_g", ple_norm_g), ("gate_b", ple_gate_b)):
        put(name, columns(A(v)))
    lora_mu = z(P, 4)
    lora_mu[:LORA, 0] = mu[lora0:lora0 + LORA]
    lora_mu[:LORA, 1] = mu[lora0 + LORA:lora0 + 2 * LORA]
    lora_mu[:, 2:] = columns(mu[lora0 + 2 * LORA:])
    put("mu", lora_mu)
    par[LORA:LORA + 16, PAR["f_bias"][0]] = A(fgate_b)
    put("q_g", np.concatenate([A(q_norm_g)] * 2)[:, None])
    put("k_g", np.concatenate([A(k_norm_g)] * 2)[:, None])
    per_feature = [mu[RW:2 * RW], mu[:RW], mu[2 * RW:3 * RW], A(k_k), A(k_a), A(r_k).reshape(RW), A(w0), A(a0),
                   A(lnx_g), A(lnx_b)]
    g_params = np.stack([v.reshape(GROUPS, 2, P) for v in per_feature], -1).transpose(0, 2, 1, 3)

    i, j = np.arange(P)[:, None], np.arange(P)[None, :]
    mats = [i == j, np.ones((P, P)), i // HD == j // HD, i < j, i <= j]
    mats += [(i >> (m + 1) == j >> (m + 1)) & ((i >> m) & 1 == 0) & ((j >> m) & 1 == 1) for m in range(LEVELS + 1)]
    col = z(P, 8)
    col[:, :3] = [RMS_EPS, GN_EPS, 8 * math.log(2.0)]
    consts = np.concatenate([m.astype(np.float32) for m in mats] + [col], 1)
    import ml_dtypes
    id16 = np.concatenate([(i == j).astype(np.float32), np.where(j > i, np.float32(-1e30), np.float32(0))], 1
                          ).astype(ml_dtypes.bfloat16)

    arrays = {
        "xT": A(x).T.reshape(KT, P, SEQ), "pT": A(p)[0].T.reshape(2, P, SEQ).transpose(1, 0, 2),
        "w_mix": w_mix, "w_gu": gu, "w_down": down, "ple_proj": proj, "ple_gate": tiles(A(ple_gate_w)),
        "w2": A(w2).reshape(LORA, GROUPS, 2 * P).transpose(1, 0, 2),
        "a2": A(a2).reshape(LORA, GROUPS, 2 * P).transpose(1, 0, 2),
        "g2": A(g2).reshape(2, P, GROUPS, 2 * P).transpose(2, 1, 0, 3),
        "params": par, "g_params": g_params, "consts": consts, "id16": id16,
    }
    arrays = {k: np.ascontiguousarray(v) for k, v in arrays.items()}
    nc = bacc.Bacc("TRN2", target_bir_lowering=False, num_devices=1)
    d = {k: nc.dram_tensor(k, v.shape, mybir.dt.from_np(v.dtype), kind="ExternalInput").ap()
         for k, v in arrays.items()}
    d["out"] = nc.dram_tensor("out", [KT, P, SEQ], F32, kind="ExternalOutput").ap()
    layer(nc, d)
    r = run_bass_kernel_spmd(nc, [arrays], core_ids=[0])
    return r.results[0]["out"].reshape(D_MODEL, SEQ).T[None].copy()
```

```python
import math

import concourse.bass as bass
from concourse import mybir

F32 = mybir.dt.float32
F32R = mybir.dt.float32r
BF16 = mybir.dt.bfloat16
U32 = mybir.dt.uint32
ALU = mybir.AluOpType
ACT = mybir.ActivationFunctionType
AX = mybir.AxisListType

P = 128
SEQ = 512
D_MODEL = 2048
KT = D_MODEL // P
HALF = KT // 2
TT = SEQ // P
HD = 64
GROUPS = 4
GH = 4
LORA = 96
LORA_SLABS = 4
GROUP_SLABS = 12
IN_SLABS = LORA_SLABS + GROUPS * GROUP_SLABS
OUT_SLABS = D_MODEL // P
D_FF = 5632
CHUNKS = 4
CF = D_FF // P // CHUNKS
DOWN_HALVES = (6, CF - 6)
N_OUT = IN_SLABS
N_FFN = N_OUT + OUT_SLABS
CHUNK_SLABS = 2 * CF + OUT_SLABS
N_PROJ = N_FFN + CHUNKS * CHUNK_SLABS
PROJ_SLABS = 2
PROJ_TILES = 8
N_GATE = N_PROJ + PROJ_SLABS
TILE_GATE = N_PROJ + PROJ_SLABS * PROJ_TILES
LEVELS = 6
ROUND_AT, SUBTRACT_AT = ((0, 8), (0, 3)), ((0, 8), (2, 4))
ITEMS_START, ITEM_STEPS = 5, 5
PARTS = {"scores": 0, "exp": 1, "scale": 2, "turn": 7, "values": 9}
FILL_STAGES, R0_STAGE, U_STAGE, Y_STAGE, TURN_STAGE = (7, 9, 11, 13, 15, 18), 11, 18, 19, 23
STAGES = 24
NORM_X, NORM_FFN, NORM_GATE, NORM_E = 1, 2, 3, 4
DECAY = math.exp(-0.5)
RMS_EPS, GN_EPS = 1e-6, 64e-5
C_ID, C_ONE, C_BLK, C_STRICT, C_INCL, C_LEVEL, C_COL = [P * i for i in (0, 1, 2, 3, 4, 5, 5 + LEVELS + 1)]
PAR = {}
for _name, _width in (("attn_g", 16), ("ffn_g", 16), ("gate_g", 16), ("ple_g", 16), ("gate_b", 16),
                      ("mu", 4), ("f_bias", 1), ("q_g", 1), ("k_g", 1)):
    PAR[_name] = (sum(w for _, w in PAR.values()), _width)
N_PAR = sum(w for _, w in PAR.values())
MU_K, MU_R, MU_V, K_K, K_A, R_K, W0, A0, LN_G, LN_B = range(10)
NG_PAR = 10


def after(eng, sem, value):
    if not (isinstance(value, int) and value <= 0):
        eng.wait_ge(sem, value)


def layer(nc, d):
    sems = {}

    def S(name):
        if name not in sems:
            sems[name] = nc.alloc_semaphore(name)
        return sems[name]

    scratch = {}

    def own_wait(eng, place=1):
        t = scratch[eng.engine]
        if eng.engine == mybir.EngineType.DVE:
            nc.vector.memset(t[:, place:place + 1], 0.0)
        elif eng.engine == mybir.EngineType.Pool:
            nc.gpsimd.tensor_tensor(t[:, place:place + 1], t[:, 0:1], t[:, 0:1], ALU.add)
        else:
            nc.scalar.activation(t[:, 1:2], t[:, 0:1], ACT.Copy)

    f32 = lambda name, shape: nc.dram_tensor(name, shape, F32)
    y_dram = f32("y_scratch", [KT, P, SEQ]).ap()
    c_dram = f32("c_scratch", [2, 16, SEQ]).ap()

    at = [(nc.sbuf_base + 63) // 64 * 64]

    def sb(name, shape, dt=F32):
        size = math.prod(shape[1:]) * (2 if dt == BF16 else 4)
        t = nc.alloc_sbuf_tensor_at(name, shape, dt, offset=at[0])
        at[0] += (size + 31) // 32 * 32
        assert at[0] <= nc.sbuf_usable_end, (name, at[0], nc.sbuf_usable_end)
        return t

    raw = sb("raw", [P, 2, HALF * P])
    w_hi = sb("w_hi", [P, 4, HALF * P], F32R)
    w_lo = sb("w_lo", [P, 4, HALF * P], F32R)
    par = sb("par", [P, N_PAR])
    ccol = sb("ccol", [P, 8])
    ones = sb("ones", [P, P])
    for _e, _n in ((mybir.EngineType.DVE, "dve"), (mybir.EngineType.Pool, "pool"), (mybir.EngineType.Activation, "act")):
        scratch[_e] = sb("scratch_" + _n, [P, 8])
    qg8 = sb("qg8", [P, 1])
    first = at[0]
    in_hi = sb("in_hi", [P, KT, SEQ], F32R)
    in_lo = sb("in_lo", [P, KT, SEQ], F32R)
    shared = at[0]
    at[0] = first
    act_hi = sb("act_hi", [P, CF, SEQ], F32R)
    act_lo = sb("act_lo", [P, CF, SEQ], F32R)
    gate_s = sb("gate_s", [P, SEQ])
    up_s = sb("up_s", [P, SEQ])
    silu_s = sb("silu_s", [P, SEQ])
    p_raw = sb("p_raw", [P, 2, SEQ])
    p_hi = sb("p_hi", [P, 2, SEQ], F32R)
    p_lo = sb("p_lo", [P, 2, SEQ], F32R)
    assert at[0] <= shared
    at[0] = first
    e_t = sb("e_t", [P, KT, SEQ])
    acc_e = sb("acc_e", [P, SEQ])
    rstd_e = sb("rstd_e", [P, SEQ])
    sq_e = sb("sq_e", [P, 2, SEQ])
    assert at[0] - first <= 2 * CF * SEQ * 4
    at[0] = shared
    h_t = sb("h_t", [P, KT, SEQ])
    hn_hi = sb("hn_hi", [P, KT, SEQ], F32R)
    hn_lo = sb("hn_lo", [P, KT, SEQ], F32R)
    sq_s = sb("sq_s", [P, SEQ])
    acc_h = sb("acc_h", [P, SEQ])
    rstd_h = sb("rstd_h", [P, SEQ])
    at[0] = shared
    consts = sb("consts", [P, C_COL + 8])
    id16 = sb("id16", [P, 2 * P], BF16)
    rstd_x = sb("rstd_x", [P, SEQ])
    acc_x = sb("acc_x", [P, 2, SEQ])
    tanh_w = sb("tanh_w", [P, SEQ])
    xa_t = sb("xa_t", [P, SEQ])
    sig_g = sb("sig_g", [P, 2, SEQ])
    work = at[0]
    x_raw = sb("x_raw", [P, KT, SEQ])
    sqx = sb("sqx", [P, 4, SEQ])
    at[0] = work
    g_par = sb("g_par", [P, 2, NG_PAR])
    w2a2 = sb("w2a2", [P, 2, 2 * P])
    g2_t = sb("g2_t", [P, 2, 2 * P])
    u_t = sb("u_t", [P, SEQ + 1])
    t1 = sb("t1", [P, SEQ])
    t2 = sb("t2", [P, SEQ])
    A_t = sb("A_t", [P, 2, SEQ])
    B_t = sb("B_t", [P, 2, SEQ])
    K_t = sb("K_t", [P, 2, SEQ])
    R_t = sb("R_t", [P, 2, SEQ])
    bonus = sb("bonus", [P, 2, SEQ])
    v_tok = sb("v_tok", [P, TT, 2 * P])
    state = sb("state", [P, 2, P])
    st_scale = sb("st_scale", [P, 2, TT])
    mid = sb("mid", [P, TT])
    q_aug = sb("q_aug", [P, GH, SEQ])
    k_aug = sb("k_aug", [P, GH, SEQ])
    fv_tok = sb("fv_tok", [P, TT, 2 * P])
    small = sb("small", [P, 64])
    stats_t = sb("stats_t", [P, GH, 6])
    o_t = sb("o_t", [P, 2, SEQ])
    overlay = at[0]
    sg_t = sb("sg_t", [P, SEQ])
    a_t = sb("a_t", [P, SEQ])
    d_t = sb("d_t", [P, SEQ])
    pi_t = sb("pi_t", [P, SEQ])
    probs = sb("probs", [P, 2, SEQ])
    probs_T = sb("probs_T", [P, TT, SEQ])
    at[0] = overlay + 4 * 4 * SEQ
    cf = sb("cf", [P, 2, SEQ])
    at[0] = overlay
    LM = sb("LM", [P, 2, 2, 2, P])
    RM = sb("RM", [P, 2, 2, 2, P])
    LTm = sb("LTm", [P, 2, GH, P])
    T_inv = sb("T_inv", [P, GH, P])
    T_invT = sb("T_invT", [P, GH, P])
    X_t = sb("X_t", [P, GH, P])
    bk_tok = sb("bk_tok", [P, 4, P])
    R0_t = sb("R0_t", [P, GH * HD])
    U_t = sb("U_t", [P, GH * HD])
    Yn_t = R0_t

    psum = [nc.alloc_psum_tensor(f"bank{i}", [P, SEQ], F32) for i in range(8)]
    aux, b3, b4, b5, b6, b7 = psum[2:]

    def gain_of(name):
        a, w = PAR[name]
        return par[:, a:a + w]

    def const(c, n=P):
        return consts[:, c:c + n]

    def over_heads(c):
        return consts[:, c:c + P].unsqueeze(1).to_broadcast([P, GH, P])

    blocks = lambda ap, m, odd: ap.rearrange("p h (n two c) -> p (h n) two c", two=2, c=1 << m)[:, :, odd, :]
    by_parity = lambda ap: ap.rearrange("p (a f) c -> p a f c", a=2)

    CB_RMS, CB_GN, CB_KK = range(3)
    cb = lambda i: ccol[:, i:i + 1]

    raw_landed = [S("raw_landed_first_half"), S("raw_landed_second_half")]
    hi_ready, lo_ready, weights_used = S("hi_ready"), S("lo_ready"), S("weights_used")
    tile_evacuated = S("tile_evacuated")

    ring_slots = lambda n_par, half: 2 * n_par + half

    def load_slab(sp, n, src, cols=(HALF * P, HALF * P), start=0):
        for half in range(2):
            after(sp, lo_ready, 2 * n + half - 1)
            sp.dma_start(raw[:, half, 0:cols[half]], src[:, sum(cols[:half]):sum(cols[:half + 1])]
                         ).then_inc(raw_landed[half], 16)

    def round_slab(act, n, par2, cols=(HALF * P, HALF * P), halves=(0, 1)):
        for half in halves:
            act.wait_ge(raw_landed[half], 16 * (n + 1))
            after(act, weights_used, 2 * n + half - 3)
            nc.scalar.activation(w_hi[:, ring_slots(par2, half), 0:cols[half]], raw[:, half, 0:cols[half]],
                                 ACT.Copy).then_inc(hi_ready, 1)

    def subtract_slab(dve, n, par2, cols=(HALF * P, HALF * P), halves=(0, 1)):
        for half in halves:
            dve.wait_ge(hi_ready, 2 * n + half + 1)
            s = ring_slots(par2, half)
            nc.vector.tensor_tensor(w_lo[:, s, 0:cols[half]], raw[:, half, 0:cols[half]],
                                    w_hi[:, s, 0:cols[half]].bitcast(F32), ALU.subtract).then_inc(lo_ready, 1)

    def three_products(out, s, col, x_hi, x_lo, start, stop):
        w_h, w_l = w_hi[:, s, col:col + P], w_lo[:, s, col:col + P]
        nc.tensor.matmul(out, w_h, x_hi, start=start, stop=False, skip_group_check=True)
        nc.tensor.matmul(out, w_h, x_lo, start=False, stop=False, skip_group_check=True)
        return nc.tensor.matmul(out, w_l, x_hi, start=False, stop=stop, skip_group_check=True)

    def multiply_slab(pe, n, par2, x_hi, x_lo, kts=(HALF, HALF), side=None, input_ready=None):
        after(pe, tile_evacuated, n - 1)
        kt = 0
        for half in range(2):
            pe.wait_ge(lo_ready, 2 * n + half + 1)
            for k in range(kts[half]):
                if side is not None:
                    side(kt)
                if input_ready is not None:
                    input_ready(kt)
                last = three_products(psum[par2][:], ring_slots(par2, half), k * P, x_hi[:, kt, :], x_lo[:, kt, :],
                                      kt == 0, kt == sum(kts) - 1)
                kt += 1
            last.then_inc(weights_used, 1)

    bank_b = [b3, b4, b5, b6, b7]
    s_bank = [b3, b4]
    pt_bank = [b5, b6]
    hp = lambda j: slice(HD * (j % 2), HD * (j % 2) + HD)
    tok = lambda tt: slice(tt * P, (tt + 1) * P)

    def pe_rwkv_prep(pe, s, kt, g):
        ft, kind = s // 3, s % 3
        f = 2 * g + ft
        if kind == 0 and kt == 8:
            if ft == 0:
                pe.wait_ge(S("g_weights_landed"), 32 * (g + 1))
                pe.wait_ge(S("tanh_ready"), 1)
                pe.wait_ge(S("xa_ready"), 1)
                if not (isinstance(g, int) and g == 0):
                    pe.wait_ge(S("y_rwkv_ready"), 2 * g)
                else:
                    pe.wait_ge(S("norm_ready"), NORM_X)
            else:
                pe.wait_ge(S("v_tok_ready"), f)
            nc.tensor.matmul(aux[:], w2a2[0:LORA, 0, tok(ft)], tanh_w[0:LORA, :], start=True, stop=True
                             ).then_inc(S("z_done"), 1)
        if kind == 0 and kt == 10:
            pe.wait_ge(S("sigmoid_z_ready"), f + 1)
            nc.tensor.matmul(aux[:], w2a2[0:LORA, 1, tok(ft)], xa_t[0:LORA, :], start=True, stop=True
                             ).then_inc(S("a_done"), 1)
        if kind == 1 and kt == 5:
            pe.wait_ge(S("k_square_ready"), f + 1)
            pe.wait_ge(S("a_ready"), f + 1)
            nc.tensor.matmul(aux[:], const(C_BLK), t1[:], start=True, stop=True).then_inc(S("k_sum_done"), 1)
        if kind == 2 and kt == 4:
            pe.wait_ge(S("rk_ready"), f + 1)
            pe.wait_ge(S("k_sum_ready"), f + 1)
            nc.tensor.matmul(aux[:], const(C_BLK), t1[:], start=True, stop=True).then_inc(S("bonus_done"), 1)
        if s == 3 and kt == 4:
            pe_values(pe, 2 * g)

    def pe_values(pe, f):
        pe.wait_ge(S("v_mixed"), f + 1)
        pe.wait_ge(S("bonus_ready"), f + 1)
        for tt in range(TT):
            last = nc.tensor.transpose(aux[:, tok(tt)], t2[:, tok(tt)], const(C_ID))
        last.then_inc(S("v_turned"), 1)

    def pe_fox_values(pe, g, ft):
        pe.wait_ge(tile_evacuated, LORA_SLABS + GROUP_SLABS * g + GROUP_SLABS - 1 + ft)
        for tt in range(TT):
            last = nc.tensor.transpose(aux[:, tok(tt)], u_t[:, 1 + tt * P:1 + (tt + 1) * P], const(C_ID))
        last.then_inc(S("fox_v_turned"), 1)

    def pe_fox_prep(pe, s, kt, g):
        if kt != 4 or s < 6:
            return
        if s == 6:
            pe_values(pe, 2 * g + 1)
            return
        c = s - 7
        if c < 4:
            pe.wait_ge(S("fox_square_ready"), 4 * g + c + 1)
            if c == 0:
                pe.wait_ge(S("v_tok_ready"), 2 * g + 2)
            else:
                pe.wait_ge(S("fox_rstd_ready"), 4 * g + c)
            nc.tensor.matmul(aux[:], const(C_BLK), t1[:], start=True, stop=True).then_inc(S("fox_sum_done"), 1)
        else:
            pe.wait_ge(S("fox_rstd_ready"), 4 * g + 4)
            pe_fox_values(pe, g, 0)

    def pe_finish(pe, s, kt, gp):
        if s == 0 and kt == 2:
            pe.wait_ge(S("fox_v_tok_ready"), 2 * gp + 1)
            pe_fox_values(pe, gp, 1)
        if s == 0 and kt in (4, 6):
            ft = (kt - 4) // 2
            if ft == 0:
                pe.wait_ge(S("g2_landed"), 16 * (gp + 1))
                pe.wait_ge(S("sig_g_ready"), 2)
                pe.wait_ge(S("fox_v_tok_ready"), 2 * gp + 2)
            else:
                pe.wait_ge(S("y_rwkv_ready"), 2 * gp + 1)
            for k in range(2):
                last = nc.tensor.matmul(aux[:], g2_t[:, k, tok(ft)], sig_g[:, k, :], start=k == 0, stop=k == 1)
            last.then_inc(S("g_done"), 1)

    def attention_item(s, kt, part):
        st = KT * s + kt - ITEMS_START - PARTS[part]
        return st // ITEM_STEPS if st % ITEM_STEPS == 0 and 0 <= st < 4 * TT * ITEM_STEPS else None

    def pe_attention(pe, s, kt, gp):
        q = attention_item(s, kt, "scores")
        if q is not None:
            j, i = q // TT, q % TT
            if q == 0:
                pe.wait_ge(S("fox_qk_ready"), 4 * gp + 4)
                pe.wait_ge(S("c_rows_landed"), 32 * (gp + 1))
                pe.wait_ge(S("y_norm_ready"), 4 * gp + 4)
            if q == 1:
                pe.wait_ge(S("X_ready"), LEVELS * (4 * gp + 4))
                pe.wait_ge(S("state_ready"), 4 * gp + 4)
            if q >= 2:
                pe.wait_ge(S("probs_ready"), 16 * gp + q - 1)
            n = (i + 1) * P
            bank = s_bank[q % 2]
            nc.tensor.matmul(bank[:, 0:n], q_aug[0:HD + 2, j, tok(i)], k_aug[0:HD + 2, j, 0:n],
                             start=True, stop=False, skip_group_check=True)
            nc.tensor.matmul(bank[:, tok(i)], id16[:, 0:P], id16[:, P:2 * P],
                             start=False, stop=True, skip_group_check=True).then_inc(S("scores_done"), 1)
        q = attention_item(s, kt, "turn")
        if q is not None:
            i = q % TT
            pe.wait_ge(S("probs_normed"), 16 * gp + q + 1)
            if q == 0:
                pe.wait_ge(S("y_turned_ready"), 4 * gp + 4)
            if q == 1:
                pe.wait_ge(S("TT_ready"), LEVELS * (4 * gp + 4))
            if q >= 2:
                pe.wait_ge(S("probs_T_ready"), 16 * gp + q - 1)
            for kb in range(i + 1):
                last = nc.tensor.transpose(pt_bank[q % 2][:, tok(kb)], probs[:, q % 2, tok(kb)], const(C_ID))
            last.then_inc(S("probs_turned"), 1)
        q = attention_item(s, kt, "values")
        if q is not None and q % TT == TT - 1:
            j = q // TT
            pe.wait_ge(S("probs_T_ready"), 16 * gp + q + 1)
            if j == 0:
                pe.wait_ge(S("fox_v_tok_ready"), 2 * gp + 2)
                pe.wait_ge(S("U_ready"), 4 * gp + 4)
            if j == 2:
                pe.wait_ge(S("o_ready"), 2 * gp + 1)
            for kb in range(TT):
                last = nc.tensor.matmul(b7[hp(j), kb * P:SEQ], fv_tok[:, kb, j * HD:(j + 1) * HD],
                                        probs_T[:, kb, kb * P:SEQ], start=kb == 0, stop=kb == TT - 1,
                                        skip_group_check=True)
            last.then_inc(S("pv_done"), 1)

    def stage_of(s, kt):
        st = 16 * (s - 6) + kt
        return st // STAGES, st % STAGES

    place = lambda j: 2 * (j % 2) + j // 2

    def grams(bank, rhs, tt, odd):
        for n, lhs in enumerate((B_t, K_t)):
            for ft in range(2):
                last = nc.tensor.matmul(bank[:, tok(2 * n + ft)], lhs[hp(odd), ft, tok(tt)],
                                        rhs[hp(odd), ft, tok(tt)], start=True, stop=True, skip_group_check=True)
        return last

    def pe_recurrence(pe, s, kt, g):
        tt, k = stage_of(s, kt)
        b = 4 * g + tt
        later = not (isinstance(g, int) and g == 0)
        if k == 0:
            pe.wait_ge(S("K_ready"), 2 * g + 2)
            if tt == 0:
                if later:
                    pe.wait_ge(S("probs_ready"), 16 * g)
                    pe.wait_ge(S("probs_T_ready"), 16 * g)
            else:
                pe.wait_ge(S("TT_ready"), LEVELS * b)
            for n, (src, ft) in enumerate(((B_t, 0), (B_t, 1), (K_t, 0), (K_t, 1))):
                last = nc.tensor.transpose(b6[:, tok(n)], src[:, ft, tok(tt)], const(C_ID))
            last.then_inc(S("bk_turned"), 1)
        if k == 1:
            if tt > 0:
                pe.wait_ge(S("state_ready"), b + 1)
            grams(b4, A_t, tt, 0).then_inc(S("LM_done"), 1)
        if k == 2:
            if tt > 0:
                pe.wait_ge(S("y_turned_ready"), b)
            grams(b5, A_t, tt, 1).then_inc(S("LM_done"), 1)
        if k == 3:
            pe.wait_ge(S("R_ready"), 2 * g + 2)
            pe.wait_ge(S("bk_tok_ready"), b + 1)
            grams(b6, R_t, tt, 0).then_inc(S("RM_done"), 1)
        if k == 4:
            if tt == 0 and later:
                pe.wait_ge(S("o_ready"), 2 * g)
            grams(b7, R_t, tt, 1).then_inc(S("RM_done"), 1)
        if k == 5:
            pe.wait_ge(S("TT0_ready"), b + 1)
            if tt > 0:
                pe.wait_ge(S("y_norm_ready"), b)
            for j in range(GH):
                last = nc.tensor.transpose(b3[:, tok(j)], T_invT[:, j, :], const(C_ID))
            last.then_inc(S("T0_done"), 1)
        if k in FILL_STAGES:
            n = 2 * FILL_STAGES.index(k)
            if n == 0:
                pe.wait_ge(S("RM_ready"), 2 * b + 2)
                pe.wait_ge(S("v_tok_ready"), 2 * g + 2)
                pe.wait_ge(S("state_ready"), b + 1)
            if n == 6:
                pe.wait_ge(S("T_ready"), LEVELS * b + 1)
            for i in (n, n + 1):
                outputs, ft, part = i // 6, i % 6 // 3, i % 3
                bank = b3 if outputs else b7
                if part == 0:
                    last = nc.tensor.matmul(bank[:, tok(ft)], (R_t if outputs else A_t)[:, ft, tok(tt)],
                                            state[:, ft, :], start=not (outputs and ft), stop=False,
                                            skip_group_check=True)
                else:
                    j = 2 * ft + part - 1
                    v = slice(j * HD, (j + 1) * HD)
                    last = nc.tensor.matmul(bank[:, v], (RM if outputs else LM)[:, j % 2, 1, ft, :], v_tok[:, tt, v],
                                            start=False, stop=not outputs, skip_group_check=True)
            if n == 4:
                last.then_inc(S("R0_done"), 1)
        if 6 <= k < 6 + 2 * LEVELS:
            m, part = (k - 6) // 2 + 1, (k - 6) % 2
            if part == 0:
                pe.wait_ge(S("LT_level_ready"), LEVELS * b + m)
                pe.wait_ge(S("T_ready"), LEVELS * b + m)
                for j in range(GH):
                    last = nc.tensor.matmul(b4[:, tok(j)], LTm[:, (m - 1) % 2, j, :], T_inv[:, j, :],
                                            start=True, stop=True, skip_group_check=True)
                last.then_inc(S("X_done"), 1)
            else:
                pe.wait_ge(S("X_ready"), LEVELS * b + m)
                if m > 1:
                    pe.wait_ge(S("TT_ready"), LEVELS * b + m - 1)
                else:
                    pe.wait_ge(S("LM_ready"), 2 * b + 2)
                    pe.wait_ge(S("RM_ready"), 2 * b + 1)
                if m < LEVELS:
                    for j in range(GH):
                        last = nc.tensor.matmul(b5[:, tok(j)], T_invT[:, j, :], X_t[:, j, :],
                                                start=True, stop=True, skip_group_check=True)
                    last.then_inc(S("dT_done"), 1)
                for j in range(GH):
                    last = nc.tensor.matmul(b6[:, tok(j)], X_t[:, j, :], T_invT[:, j, :],
                                            start=True, stop=True, skip_group_check=True)
                last.then_inc(S("dTT_done"), 1)
        if k == U_STAGE:
            pe.wait_ge(S("R0_ready"), b + 1)
            pe.wait_ge(S("TT_ready"), LEVELS * b + LEVELS)
            for j in range(GH):
                last = nc.tensor.matmul(b7[:, GH * HD + j * HD:GH * HD + (j + 1) * HD], T_invT[:, place(j), :],
                                        R0_t[:, j * HD:(j + 1) * HD], start=True, stop=True, skip_group_check=True)
            last.then_inc(S("U_done"), 1)
        if k == Y_STAGE:
            pe.wait_ge(S("U_ready"), b + 1)
            for j in range(GH):
                v = slice(j * HD, (j + 1) * HD)
                last = nc.tensor.matmul(b3[:, v], RM[:, j % 2, 0, j // 2, :], U_t[:, v], start=False, stop=True,
                                        skip_group_check=True)
            last.then_inc(S("Y_done"), 1)
            if tt < TT - 1:
                for ft in range(2):
                    nc.tensor.matmul(b4[:, tok(ft)], bk_tok[:, ft, :], U_t[:, tok(ft)],
                                     start=True, stop=False, skip_group_check=True)
                    last = nc.tensor.matmul(b4[:, tok(ft)], bk_tok[:, 2 + ft, :], v_tok[:, tt, tok(ft)],
                                            start=False, stop=True, skip_group_check=True)
                last.then_inc(S("state_step_done"), 1)
        if k == TURN_STAGE:
            pe.wait_ge(S("y_norm_ready"), b + 1)
            for ft in range(2):
                last = nc.tensor.transpose(b5[:, tok(ft)], Yn_t[:, tok(ft)], const(C_ID))
            last.then_inc(S("y_turned"), 1)

    def act_rwkv_prep(act, s, kt, g):
        ft, kind = s // 3, s % 3
        f = 2 * g + ft
        gp_col = lambda c: g_par[:, ft, c:c + 1]
        if kind == 0 and kt == 8:
            act.wait_ge(S("z_done"), f + 1)
            act.wait_ge(S("g_par_landed"), 16 * (g + 1))
            nc.scalar.activation(sg_t[:], aux[:], ACT.Sigmoid, bias=gp_col(W0)).then_inc(S("sigmoid_z_ready"), 1)
        if kind == 0 and kt == 10:
            act.wait_ge(S("a_done"), f + 1)
            nc.scalar.activation(a_t[:], aux[:], ACT.Sigmoid, bias=gp_col(A0)).then_inc(S("a_ready"), 1)
        if kind == 0 and kt == 12:
            act.wait_ge(S("d_ready"), f + 1)
            act.wait_ge(S("st_exponent_ready"), f + 1)
            act.wait_ge(S("d_prev_ready"), f + 1)
            nc.scalar.activation(pi_t[:], d_t[:], ACT.Exp, scale=DECAY).then_inc(S("inverse_decay_ready"), 1)
            act.wait_ge(S("inverse_decay_ready"), f + 1)
            nc.scalar.activation(d_t[:], d_t[:], ACT.Exp, scale=-DECAY)
            nc.scalar.activation(sg_t[:], sg_t[:], ACT.Exp, scale=-DECAY)
            nc.scalar.activation(st_scale[:, ft, 0:TT - 1], small[:, 0:TT - 1], ACT.Exp,
                                 scale=-DECAY).then_inc(S("decays_ready"), 1)
        if kind == 1 and kt == 1:
            act.wait_ge(S("k_mixed"), f + 1)
            nc.scalar.activation(t1[:], t2[:], ACT.Square, scale=gp_col(K_K)).then_inc(S("k_square_ready"), 1)
        if kind == 1 and kt == 6:
            act.wait_ge(S("k_sum_ready"), f + 1)
            nc.scalar.activation(t1[:], t1[:], ACT.Ln, scale=2.0 ** 16).then_inc(S("k_log_ready"), 1)
            act.wait_ge(S("k_log_ready"), f + 1)
            nc.scalar.activation(t1[:], t1[:], ACT.Exp, scale=-0.5, bias=cb(CB_KK)).then_inc(S("k_rnorm_ready"), 1)
        if kind == 2 and kt == 5:
            act.wait_ge(S("bonus_done"), f + 1)
            if not (isinstance(g, int) and g == 0):
                act.wait_ge(S("y_plus_bonus"), 2 * g)
            nc.scalar.activation(bonus[:, ft, :], aux[:], ACT.Copy).then_inc(S("bonus_ready"), 1)
        if s == 3 and kt == 5:
            act_values(act, g, 0)

    def act_values(act, g, ft):
        act.wait_ge(S("v_turned"), 2 * g + ft + 1)
        nc.scalar.activation(v_tok[:, :, tok(ft)], aux[:].rearrange("p (t c) -> p t c", t=TT), ACT.Copy
                             ).then_inc(S("v_tok_ready"), 1)

    def act_fox_values(act, gf, ft):
        act.wait_ge(S("fox_v_turned"), gf + 1)
        nc.scalar.activation(fv_tok[:, :, tok(ft)], aux[:].rearrange("p (t c) -> p t c", t=TT), ACT.Copy
                             ).then_inc(S("fox_v_tok_ready"), 1)

    def act_fox_prep(act, s, kt, g):
        if s == 6 and kt == 5:
            act_values(act, g, 1)
        c = s - 7
        if 0 <= c < 4 and kt == 2:
            act.wait_ge(tile_evacuated, LORA_SLABS + GROUP_SLABS * g + s)
            nc.scalar.activation(t1[:], u_t[:, 1:SEQ + 1], ACT.Square).then_inc(S("fox_square_ready"), 1)
        if 0 <= c < 4 and kt == 5:
            act.wait_ge(S("fox_sum_done"), 4 * g + c + 1)
            nc.scalar.activation(t2[:], aux[:], ACT.Ln, scale=1.0 / HD, bias=cb(CB_RMS)
                                 ).then_inc(S("fox_log_ready"), 1)
            act.wait_ge(S("fox_log_ready"), 4 * g + c + 1)
            nc.scalar.activation(t2[:], t2[:], ACT.Exp, scale=-0.5).then_inc(S("fox_rstd_ready"), 1)
        if c == 4 and kt == 5:
            act_fox_values(act, 2 * g, 0)

    def act_finish(act, s, kt, gp):
        if s == 0 and kt == 2:
            act_fox_values(act, 2 * gp + 1, 1)

    def act_attention(act, s, kt, gp):
        q = attention_item(s, kt, "exp")
        if q is not None:
            n = (q % TT + 1) * P
            act.wait_ge(S("max_ready"), 16 * gp + q + 1)
            if q >= 2:
                act.wait_ge(S("probs_turned"), 16 * gp + q - 1)
            nc.scalar.activation(probs[:, q % 2, 0:n], s_bank[q % 2][:, 0:n], ACT.Exp,
                                 bias=small[:, 8 + q % 2:9 + q % 2], accum_out=small[:, 10 + q % 2:11 + q % 2]
                                 ).then_inc(S("probs_ready"), 1)
        q = attention_item(s, kt, "turn")
        if q is not None:
            j, i = q // TT, q % TT
            n = (i + 1) * P
            act.wait_ge(S("probs_turned"), 16 * gp + q + 1)
            if i == 0 and j > 0:
                act.wait_ge(S("pv_done"), 4 * gp + j)
            nc.scalar.activation(probs_T[:, 0:i + 1, tok(i)],
                                 pt_bank[q % 2][:, 0:n].rearrange("p (k c) -> p k c", c=P), ACT.Copy
                                 ).then_inc(S("probs_T_ready"), 1)

    def act_recurrence(act, s, kt, g):
        tt, k = stage_of(s, kt)
        b = 4 * g + tt
        v4 = lambda bank: bank[:].rearrange("p (h c) -> p h c", h=GH)
        if k == 0:
            act.wait_ge(S("bk_turned"), b + 1)
            if tt > 0:
                act.wait_ge(S("state_step_done"), 3 * g + tt)
            nc.scalar.activation(bk_tok[:], v4(b6), ACT.Copy).then_inc(S("bk_tok_ready"), 1)
        if k == 5:
            act.wait_ge(S("T0_done"), b + 1)
            nc.scalar.activation(T_inv[:], v4(b3), ACT.Copy).then_inc(S("T_ready"), 1)
        if 6 <= k < 6 + 2 * LEVELS and (k - 6) % 2 == 0:
            m = (k - 6) // 2 + 1
            act.wait_ge(S("X_done"), LEVELS * b + m)
            nc.scalar.activation(X_t[:], v4(b4), ACT.Copy).then_inc(S("X_ready"), 1)
        if k == R0_STAGE:
            act.wait_ge(S("R0_done"), b + 1)
            nc.scalar.activation(R0_t[:], b7[:, 0:GH * HD], ACT.Copy).then_inc(S("R0_ready"), 1)
        if k == U_STAGE:
            act.wait_ge(S("U_done"), b + 1)
            nc.scalar.activation(U_t[:], b7[:, GH * HD:2 * GH * HD], ACT.Copy).then_inc(S("U_ready"), 1)
        if k == Y_STAGE:
            act.wait_ge(S("y_stats_ready"), b + 1)
            nc.scalar.activation(small[:, 20:24], small[:, 40:48:2], ACT.Sqrt, bias=cb(CB_GN)
                                 ).then_inc(S("y_std_ready"), 1)
        if k == TURN_STAGE:
            act.wait_ge(S("y_turned"), b + 1)
            for ft in range(2):
                ins = nc.scalar.activation(R_t[:, ft, tok(tt)], b5[:, tok(ft)], ACT.Identity,
                                           scale=g_par[:, ft, LN_G:LN_G + 1], bias=g_par[:, ft, LN_B:LN_B + 1])
            ins.then_inc(S("y_turned_ready"), 1)

    def evacuate(dve, n, par2):
        dve.wait_ge(weights_used, 2 * n + 2)
        return nc.vector.tensor_tensor(u_t[:, 1:SEQ + 1], psum[par2][:], rstd_x[:], ALU.mult)

    def dve_arrival_rwkv(dve, s, g):
        n = LORA_SLABS + GROUP_SLABS * g + s - 1
        ft, kind = (s - 1) // 3, (s - 1) % 3
        f = 2 * g + ft
        a = 6 * g + s - 1
        gp_col = lambda c: g_par[:, ft, c:c + 1]
        if s == 1 and isinstance(g, int) and g == 0:
            dve.wait_ge(S("lora_mixed"), LORA_SLABS - 1)
        if s == 1 and not (isinstance(g, int) and g == 0):
            dve.wait_ge(S("fox_v_turned"), 2 * g)
        evacuate(dve, n, (s - 1) % 2).then_inc(tile_evacuated, 1)
        if kind == 1:
            dve.wait_ge(S("K_ready"), f + 1)
        if kind == 2:
            dve.wait_ge(S("bonus_done"), f + 1)
        dve.wait_ge(tile_evacuated, n + 1)
        nc.vector.tensor_tensor(t1[:], u_t[:, 0:SEQ], u_t[:, 1:SEQ + 1], ALU.subtract).then_inc(S("shift_ready"), 1)
        if s == 1:
            dve.wait_ge(S("g_par_landed"), 16 * (g + 1))
        dve.wait_ge(S("shift_ready"), LORA_SLABS + a + 1)
        if kind == 0:
            if ft == 1:
                dve.wait_ge(S("v_turned"), f)
            after(dve, S("bonus_v_ready"), f)
            nc.vector.scalar_tensor_tensor(out=t2[:], in0=t1[:], scalar=gp_col(MU_K), in1=u_t[:, 1:SEQ + 1],
                                           op0=ALU.mult, op1=ALU.add).then_inc(S("k_mixed"), 1)
        if kind == 1:
            if ft == 0 and not (isinstance(g, int) and g == 0):
                dve.wait_ge(S("y_rwkv_stored"), 32 * g)
            nc.vector.scalar_tensor_tensor(out=R_t[:, ft, :], in0=t1[:], scalar=gp_col(MU_R),
                                           in1=u_t[:, 1:SEQ + 1], op0=ALU.mult, op1=ALU.add
                                           ).then_inc(S("r_mixed"), 1)
            dve.wait_ge(S("r_mixed"), f + 1)
            nc.vector.scalar_tensor_tensor(out=t1[:], in0=R_t[:, ft, :], scalar=gp_col(R_K), in1=t2[:],
                                           op0=ALU.mult, op1=ALU.mult).then_inc(S("rk_ready"), 1)
            dve.wait_ge(S("rk_ready"), f + 1)
            nc.vector.tensor_tensor(R_t[:, ft, :], R_t[:, ft, :], d_t[:], ALU.mult).then_inc(S("R_ready"), 1)
        if kind == 2:
            nc.vector.scalar_tensor_tensor(out=t2[:], in0=t1[:], scalar=gp_col(MU_V), in1=u_t[:, 1:SEQ + 1],
                                           op0=ALU.mult, op1=ALU.add).then_inc(S("v_mixed"), 1)
            dve.wait_ge(S("v_mixed"), f + 1)
            dve.wait_ge(S("bonus_ready"), f + 1)
            nc.vector.tensor_tensor(bonus[:, ft, :], bonus[:, ft, :], t2[:], ALU.mult).then_inc(S("bonus_v_ready"), 1)

    def dve_rwkv_prep(dve, s, kt, g):
        ft, kind = s // 3, s % 3
        f = 2 * g + ft
        gp_col = lambda c: g_par[:, ft, c:c + 1]
        if kind == 0 and kt == 9:
            dve.wait_ge(S("sigmoid_z_ready"), f + 1)
            after(dve, S("R_ready"), f)
            for tt in range(TT):
                ins = nc.vector.tensor_tensor_scan(d_t[:, tok(tt)], ones[:], sg_t[:, tok(tt)], 0.0, ALU.mult, ALU.add)
            ins.then_inc(S("scan_step"), 1)
            dve.wait_ge(S("scan_step"), 2 * f + 1)
            d3 = d_t[:].rearrange("p (t c) -> p t c", t=TT)
            nc.vector.tensor_copy(mid[:], d3[:, :, P // 2 - 1]).then_inc(S("scan_step"), 1)
            dve.wait_ge(S("scan_step"), 2 * f + 2)
            nc.vector.tensor_tensor(d3, d3, mid[:].unsqueeze(2).to_broadcast([P, TT, P]), ALU.subtract
                                    ).then_inc(S("d_ready"), 1)
            dve.wait_ge(S("d_ready"), f + 1)
            nc.vector.tensor_tensor(small[:, 0:TT - 1], d3[:, 0:TT - 1, P - 1], mid[:, 1:TT], ALU.add
                                    ).then_inc(S("st_exponent_ready"), 1)
        if kind == 1 and kt == 5:
            dve.wait_ge(S("k_sum_done"), f + 1)
            nc.vector.tensor_scalar(t1[:], aux[:], 1e-24, None, ALU.max).then_inc(S("k_sum_ready"), 1)
        if kind == 1 and kt == 9:
            dve.wait_ge(S("k_rnorm_ready"), f + 1)
            dve.wait_ge(S("decays_ready"), f + 1)
            nc.vector.scalar_tensor_tensor(out=t1[:], in0=t2[:], scalar=gp_col(K_K), in1=t1[:],
                                           op0=ALU.mult, op1=ALU.mult).then_inc(S("key_step"), 1)
            dve.wait_ge(S("key_step"), 6 * f + 1)
            nc.vector.scalar_tensor_tensor(out=A_t[:, ft, :], in0=t1[:], scalar=-1.0, in1=sg_t[:],
                                           op0=ALU.mult, op1=ALU.mult).then_inc(S("key_step"), 1)
        if kind == 1 and kt == 10:
            dve.wait_ge(S("key_step"), 6 * f + 2)
            nc.vector.tensor_tensor(t1[:], t1[:], a_t[:], ALU.mult).then_inc(S("key_step"), 1)
            dve.wait_ge(S("key_step"), 6 * f + 3)
            nc.vector.tensor_tensor(B_t[:, ft, :], t1[:], pi_t[:], ALU.mult).then_inc(S("key_step"), 1)
        if kind == 1 and kt == 11:
            nc.vector.tensor_scalar(a_t[:], a_t[:], -1.0, gp_col(K_A), ALU.add, ALU.mult
                                    ).then_inc(S("key_step"), 1)
            dve.wait_ge(S("key_step"), 6 * f + 5)
            nc.vector.scalar_tensor_tensor(out=t2[:], in0=a_t[:], scalar=1.0, in1=t2[:], op0=ALU.add, op1=ALU.mult
                                           ).then_inc(S("key_step"), 1)
        if kind == 1 and kt == 12:
            dve.wait_ge(S("key_step"), 6 * f + 6)
            nc.vector.tensor_tensor(K_t[:, ft, :], t2[:], pi_t[:], ALU.mult).then_inc(S("K_ready"), 1)

    def dve_arrival_fox(dve, s, g):
        n = LORA_SLABS + GROUP_SLABS * g + s - 1
        c = s - 7
        if c >= 1:
            if c <= 4:
                dve.wait_ge(S("fox_qk_ready"), 4 * g + c)
        if c == 5:
            dve.wait_ge(S("fox_v_turned"), 2 * g + 1)
        evacuate(dve, n, (s - 1) % 2).then_inc(tile_evacuated, 1)

    def dve_fox_prep(dve, s, kt, g):
        c = s - 7
        if 0 <= c < 4 and kt == 6:
            dve.wait_ge(S("fox_rstd_ready"), 4 * g + c + 1)
            dst, gain = (q_aug, qg8) if c < 2 else (k_aug, gain_of("k_g"))
            for hh in range(2):
                ps = slice(HD * hh, HD * hh + HD)
                ins = nc.vector.scalar_tensor_tensor(out=dst[0:HD, 2 * (c % 2) + hh, :], in0=u_t[ps, 1:SEQ + 1],
                                                     scalar=gain[ps, :], in1=t2[ps, :], op0=ALU.mult, op1=ALU.mult)
            ins.then_inc(S("fox_qk_ready"), 1)

    def dve_finish(dve, s, kt, gp):
        if s == 0 and kt in (4, 6):
            ft = (kt - 4) // 2
            dve.wait_ge(S("g_done"), 2 * gp + ft + 1)
            dve.wait_ge(S("y_plus_bonus"), 2 * gp + ft + 1)
            nc.vector.tensor_tensor(R_t[:, ft, :], R_t[:, ft, :], aux[:], ALU.mult).then_inc(S("y_rwkv_ready"), 1)

    def dve_attention(dve, s, kt, gp):
        q = attention_item(s, kt, "scores")
        if q is not None:
            dve.wait_ge(S("scores_done"), 16 * gp + q + 1)
            nc.vector.tensor_reduce(small[:, 8 + q % 2:9 + q % 2], s_bank[q % 2][:, 0:(q % TT + 1) * P], AX.X,
                                    ALU.max, negate=True).then_inc(S("max_ready"), 1)
        q = attention_item(s, kt, "scale")
        if q is not None:
            dve.wait_ge(S("probs_ready"), 16 * gp + q + 1)
            nc.vector.reciprocal(small[:, 12 + q % 2:13 + q % 2], small[:, 10 + q % 2:11 + q % 2]
                                 ).then_inc(S("rsum_ready"), 1)
        q = attention_item(s, kt, "values")
        if q is not None and q % (2 * TT) == 2 * TT - 1:
            j = q // TT
            dve.wait_ge(S("pv_done"), 4 * gp + j + 1)
            if j == 1:
                dve.wait_ge(S("o_stored"), 32 * gp + 1)
            nc.vector.tensor_copy(o_t[:, j // 2, :], b7[:]).then_inc(S("o_ready"), 1)

    def dve_recurrence(dve, s, kt, g):
        tt, k = stage_of(s, kt)
        b = 4 * g + tt
        v4 = lambda bank: bank[:].rearrange("p (h c) -> p h c", h=GH)
        if k == 0 and tt == 0:
            if not (isinstance(g, int) and g == 0):
                dve.wait_ge(S("pv_done"), 4 * g)
            dve.wait_ge(S("c_stored"), 32)
            nc.vector.memset(LM[:], 0.0).then_inc(S("grams_cleared"), 1)
            nc.vector.memset(state[:], 0.0).then_inc(S("state_ready"), 1)
            dve.wait_ge(S("grams_cleared"), g + 1)
        for kk, bank, dst, mask, name in ((1, b4, LM[:, 0], C_STRICT, "LM"), (2, b5, LM[:, 1], C_STRICT, "LM"),
                                          (3, b6, RM[:, 0], C_INCL, "RM"), (4, b7, RM[:, 1], C_INCL, "RM")):
            if k == kk:
                dve.wait_ge(S(name + "_done"), 2 * b + (kk - 1) % 2 + 1)
                if kk == 3 and tt == 0:
                    dve.wait_ge(S("RM_cleared"), g + 1)
                if kk == 1 and tt > 0:
                    dve.wait_ge(S("LT_level_ready"), LEVELS * b)
                own_wait(dve, kk)
                nc.vector.copy_predicated(dst.rearrange("p g f c -> p (g f) c"), over_heads(mask).bitcast(U32),
                                          v4(bank)).then_inc(S(name + "_ready"), 1)
            if k == kk == 2:
                dve.wait_ge(S("LM_ready"), 2 * b + 2)
                if tt > 0:
                    dve.wait_ge(S("U_done"), b)
                nc.vector.tensor_tensor(by_parity(T_invT[:]), LM[:, :, 0], by_parity(over_heads(C_LEVEL)), ALU.mult
                                        ).then_inc(S("pairs_ready"), 1)
                dve.wait_ge(S("pairs_ready"), b + 1)
                nc.vector.tensor_tensor(T_invT[:], T_invT[:], over_heads(C_ID), ALU.add).then_inc(S("TT0_ready"), 1)
        if 6 <= k < 6 + 2 * LEVELS and (k - 6) % 2 == 1:
            m = (k - 6) // 2 + 1
            if m < LEVELS:
                dve.wait_ge(S("dT_done"), (LEVELS - 1) * b + m)
                nc.vector.tensor_tensor(blocks(T_inv[:], m, 0), blocks(T_inv[:], m, 0), blocks(v4(b5), m, 0), ALU.add
                                        ).then_inc(S("T_ready"), 1)
            dve.wait_ge(S("dTT_done"), LEVELS * b + m)
            nc.vector.tensor_tensor(blocks(T_invT[:], m, 1), blocks(T_invT[:], m, 1), blocks(v4(b6), m, 1), ALU.add
                                    ).then_inc(S("TT_ready"), 1)
        if k == Y_STAGE:
            dve.wait_ge(S("Y_done"), b + 1)
            for j in range(GH):
                ins = nc.vector.bn_stats(stats_t[:, j, :], b3[:, j * HD:(j + 1) * HD])
            ins.then_inc(S("y_halves_ready"), 1)
            dve.wait_ge(S("y_halves_ready"), b + 1)
            own_wait(dve, 5)
            for j in range(GH):
                ins = nc.vector.bn_aggr(small[:, 39 + 2 * j:41 + 2 * j], stats_t[:, j, :])
            ins.then_inc(S("y_stats_ready"), 1)
            if tt < TT - 1:
                dve.wait_ge(S("state_step_done"), 3 * g + tt + 1)
                nc.vector.tensor_tensor(state[:], state[:], b4[:, 0:2 * P].rearrange("p (f c) -> p f c", f=2),
                                        ALU.add).then_inc(S("state_sum_ready"), 1)
                dve.wait_ge(S("state_sum_ready"), 3 * g + tt + 1)
                for ft in range(2):
                    ins = nc.vector.scalar_tensor_tensor(out=state[:, ft, :], in0=state[:, ft, :],
                                                         scalar=st_scale[:, ft, tt:tt + 1], in1=const(C_BLK),
                                                         op0=ALU.mult, op1=ALU.mult)
                ins.then_inc(S("state_ready"), 1)
            dve.wait_ge(S("y_std_ready"), b + 1)
            nc.vector.reciprocal(small[:, 24:28], small[:, 20:24]).then_inc(S("y_rstd_ready"), 1)
            dve.wait_ge(S("y_rstd_ready"), b + 1)
            for j in range(GH):
                v = slice(j * HD, (j + 1) * HD)
                ins = nc.vector.tensor_scalar(Yn_t[:, v], b3[:, v], small[:, 39 + 2 * j:40 + 2 * j],
                                              small[:, 24 + j:25 + j], ALU.subtract, ALU.mult)
            ins.then_inc(S("y_norm_ready"), 1)

    def pool_rwkv_prep(pool, s, kt, g):
        if s % 3 == 0 and kt == 11:
            pool.wait_ge(S("d_ready"), 2 * g + s // 3 + 1)
            nc.gpsimd.tensor_tensor(sg_t[:], d_t[:], sg_t[:], ALU.subtract).then_inc(S("d_prev_ready"), 1)

    def pool_finish(pool, s, kt, gp):
        if s == 0 and kt in (3, 5):
            ft = (kt - 3) // 2
            pool.wait_ge(S("y_turned_ready"), 4 * gp + 4)
            pool.wait_ge(S("bonus_v_ready"), 2 * gp + ft + 1)
            nc.gpsimd.tensor_tensor(R_t[:, ft, :], R_t[:, ft, :], bonus[:, ft, :], ALU.add
                                    ).then_inc(S("y_plus_bonus"), 1)

    def pool_attention(pool, s, kt, gp):
        q = attention_item(s, kt, "scale")
        if q is not None:
            n = (q % TT + 1) * P
            pool.wait_ge(S("rsum_ready"), 16 * gp + q + 1)
            own_wait(pool, 1 + q % 2)
            nc.gpsimd.tensor_scalar(probs[:, q % 2, 0:n], probs[:, q % 2, 0:n], small[:, 12 + q % 2:13 + q % 2],
                                    1.0, ALU.mult, ALU.mult).then_inc(S("probs_normed"), 1)

    def pool_recurrence(pool, s, kt, g):
        tt, k = stage_of(s, kt)
        b = 4 * g + tt
        if k == 0 and tt == 0:
            if not (isinstance(g, int) and g == 0):
                pool.wait_ge(S("pv_done"), 4 * g)
            pool.wait_ge(S("c_stored"), 32)
            pool.wait_ge(S("R_ready"), 2 * g + 2)
            own_wait(pool, 3)
            nc.gpsimd.memset(RM[:], 0.0).then_inc(S("RM_cleared"), 1)
        if k == 2:
            pool.wait_ge(S("LM_ready"), 2 * b + 2)
        if 2 <= k < 2 + 2 * LEVELS and k % 2 == 0:
            m = k // 2
            if m > 2:
                pool.wait_ge(S("X_done"), LEVELS * b + m - 2)
            nc.gpsimd.tensor_tensor(by_parity(LTm[:, (m - 1) % 2]), LM[:, :, 0],
                                    by_parity(over_heads(C_LEVEL + m * P)), ALU.mult
                                    ).then_inc(S("LT_level_ready"), 1)


    def dve_arrival_lora(dve, m):
        if m == 0:
            dve.wait_ge(S("norm_ready"), NORM_X)
        if m == 2:
            dve.wait_ge(S("xa_ready"), 1)
        if m == 3:
            dve.wait_ge(S("lora_mixed"), 2)
        evacuate(dve, m, m % 2).then_inc(tile_evacuated, 1)
        dve.wait_ge(S("shift_ready"), m + 1)
        if m == 2:
            dve.wait_ge(S("tanh_ready"), 1)
        if m == 3:
            dve.wait_ge(S("sig_g_ready"), 1)
        dst = xa_t if m == 1 else t2
        nc.vector.scalar_tensor_tensor(out=dst[:], in0=t1[:], scalar=gain_of("mu")[:, m:m + 1],
                                       in1=u_t[:, 1:SEQ + 1], op0=ALU.mult, op1=ALU.add
                                       ).then_inc(S("xa_ready") if m == 1 else S("lora_mixed"), 1)
        if m == 0:
            fs = slice(LORA, LORA + 16)
            dve.wait_ge(S("lora_mixed"), 1)
            nc.vector.tensor_scalar(cf[fs, 0, :], t2[fs, :], gain_of("f_bias")[fs, :], None, ALU.add
                                    ).then_inc(S("forget_step"), 1)
            dve.wait_ge(S("forget_step"), 1)
            nc.vector.scalar_tensor_tensor(out=cf[fs, 1, :], in0=cf[fs, 0, :], scalar=-1.0, in1=cf[fs, 0, :],
                                           op0=ALU.mult, op1=ALU.max).then_inc(S("forget_step"), 1)
            dve.wait_ge(S("forget_log_step"), 2)
            nc.vector.scalar_tensor_tensor(out=cf[fs, 1, :], in0=cf[fs, 0, :], scalar=0.0, in1=cf[fs, 1, :],
                                           op0=ALU.min, op1=ALU.subtract).then_inc(S("forget_step"), 1)
            dve.wait_ge(S("forget_step"), 3)
            for tt in range(TT):
                if tt:
                    dve.wait_ge(S("forget_step"), 3 + tt)
                nc.vector.tensor_tensor_scan(cf[fs, 0, tok(tt)], ones[fs, :], cf[fs, 1, tok(tt)],
                                             cf[fs, 0, tt * P - 1:tt * P] if tt else 0.0, ALU.mult, ALU.add
                                             ).then_inc(S("forget_step"), 1)
            dve.wait_ge(S("forget_step"), 3 + TT)
            nc.vector.tensor_scalar(cf[fs, 1, :], cf[fs, 0, :], -1.0, None, ALU.mult).then_inc(S("c_ready"), 1)

    def act_arrival_lora(act, m):
        if m == 0:
            act.wait_ge(S("lora_mixed"), 1)
            nc.scalar.activation(tanh_w[0:LORA, :], t2[0:LORA, :], ACT.Tanh).then_inc(S("tanh_ready"), 1)
            fs = slice(LORA, LORA + 16)
            act.wait_ge(S("forget_step"), 2)
            nc.scalar.activation(cf[fs, 1, :], cf[fs, 1, :], ACT.Exp, scale=-1.0).then_inc(S("forget_log_step"), 1)
            act.wait_ge(S("forget_log_step"), 1)
            nc.scalar.activation(cf[fs, 1, :], cf[fs, 1, :], ACT.Ln, bias=1.0).then_inc(S("forget_log_step"), 1)
        if m >= 2:
            act.wait_ge(S("lora_mixed"), m)
            nc.scalar.activation(sig_g[:, m - 2, :], t2[:], ACT.Sigmoid).then_inc(S("sig_g_ready"), 1)

    def pool_arrival_lora(pool, m):
        pool.wait_ge(tile_evacuated, m + 1)
        nc.gpsimd.tensor_tensor(t1[:], u_t[:, 0:SEQ], u_t[:, 1:SEQ + 1], ALU.subtract).then_inc(S("shift_ready"), 1)

    def hn_steps(gain):
        def on_act(act, o, tile, idx, norm):
            act.wait_ge(tile_evacuated, tile + 1)
            nc.scalar.activation(hn_hi[:, o, :], h_t[:, o, :], ACT.Copy, scale=gain_of(gain)[:, o_col(o)]
                                 ).then_inc(S("hn_hi_ready"), 1)
            act.wait_ge(S("h_summed"), idx + norm)
            own_wait(act)
            nc.scalar.activation(sq_s[:], h_t[:, o, :], ACT.Square).then_inc(S("h_squared"), 1)

        def on_dve(dve, o, idx):
            dve.wait_ge(S("hn_hi_ready"), idx + 1)
            nc.vector.scalar_tensor_tensor(out=hn_lo[:, o, :], in0=h_t[:, o, :], scalar=gain_of(gain)[:, o_col(o)],
                                           in1=hn_hi[:, o, :].bitcast(F32), op0=ALU.mult, op1=ALU.subtract
                                           ).then_inc(S("hn_ready"), 1)

        def on_pool(pool, idx):
            pool.wait_ge(S("h_squared"), idx + 1)
            nc.gpsimd.tensor_tensor(acc_h[:], acc_h[:], sq_s[:], ALU.add).then_inc(S("h_summed"), 1)
        return on_act, on_dve, on_pool

    def o_col(o):
        return slice(o, o + 1) if isinstance(o, int) else bass.ds(o, 1)

    ffn_norm, gate_norm = hn_steps("ffn_g"), hn_steps("gate_g")
    gate_slab_cols = (HALF * P, HALF * P)
    down_cols = tuple(k * P for k in DOWN_HALVES)

    def pairs(eng, count, body):
        with eng.Fori(0, count - 1) as i:
            body(i, False)
        body(count - 1, True)

    def group_loop(eng, group):
        group(0, None)
        with eng.Fori(0, GROUPS - 1) as i:
            group(i + 1, i)

    TAIL_TILES = [*range(6), *range(8, 14), 6, 7, 14, 15]
    cut_step = lambda i: 12 + 3 * i + 6 * (i == KT - 2) if i < KT - 1 else KT * 6
    cut_at = {cut_step(i): i for i in range(KT)}
    multiplied_at = {cut_step(i) + 5: i for i in range(KT - 1)}
    fox_tiles = KT - 2

    def tail_source(kt):
        if kt in (6, 7):
            return R_t[:, kt - 6, :]
        return o_t[:, kt - fox_tiles, :] if kt >= fox_tiles else in_lo[:, kt, :].bitcast(F32)

    def tail_steps(each):
        for st in range(6 * KT + 1):
            each(st, st // KT, st % KT)

    slab_of = lambda g, s: LORA_SLABS + GROUP_SLABS * g + s
    ffn_base = lambda c: N_FFN + CHUNK_SLABS * c
    down_base = lambda c: N_FFN + CHUNK_SLABS * c + 2 * CF

    with nc.Block() as block:

        @block.sync
        def _(sp):
            sp.dma_start(par[:], d["params"]).then_inc(S("par_landed"), 16)
            x_quarter = lambda i: d["xT"][4 * i:4 * i + 4].rearrange("k p t -> p k t")
            for i in range(4):
                if i < 2:
                    sp.dma_start(raw[:, i, :], d["w_mix"][0][:, i * HALF * P:(i + 1) * HALF * P]
                                 ).then_inc(raw_landed[i], 16)
                sp.dma_start(x_raw[:, 4 * i:4 * i + 4, :], x_quarter(i)).then_inc(S(f"input_landed_{i}"), 16)
            load_slab(sp, 1, d["w_mix"][1])
            sp.dma_start(ones[:], d["consts"][:, C_ONE:C_ONE + P]).then_inc(S("ones_landed"), 16)
            sp.dma_start(ccol[:], d["consts"][:, C_COL:C_COL + 8]).then_inc(S("ones_landed"), 16)
            sp.dma_start(consts[:], d["consts"]).then_inc(S("consts_landed"), 16)
            sp.dma_start(id16[:], d["id16"]).then_inc(S("consts_landed"), 16)

            def load_params(g):
                sp.dma_start(g_par[:], d["g_params"][g]).then_inc(S("g_par_landed"), 16)

            def load_lora(g):
                for i, w in enumerate(("w2", "a2")):
                    sp.dma_start(w2a2[0:LORA, i, :], d[w][g]).then_inc(S("g_weights_landed"), 16)

            load_slab(sp, 2, d["w_mix"][2])
            sp.wait_ge(S("in_ready"), KT)
            sp.wait_ge(S("x_summed_pool"), KT // 2)
            sp.wait_ge(S("x_summed_dve"), KT // 2)
            load_params(0)
            load_lora(0)
            for n in range(LORA_SLABS):
                if n > 0:
                    load_slab(sp, n + 2, d["w_mix"][n + 2])
                if n == 1:
                    sp.wait_ge(S("c_ready"), 1)
                    for i in range(2):
                        sp.dma_start(c_dram[i], cf[LORA:LORA + 16, i, :]).then_inc(S("c_stored"), 16)

            def store_rwkv(gp):
                sp.wait_ge(S("y_rwkv_ready"), 2 * gp + 2)
                for ft in range(2):
                    sp.dma_start(y_dram[2 * gp + ft], R_t[:, ft, :]).then_inc(S("y_rwkv_stored"), 16)

            def store_fox(gp):
                sp.wait_ge(S("o_ready"), 2 * gp + 2)
                for pr in range(2):
                    sp.dma_start(y_dram[2 * GROUPS + 2 * gp + pr], o_t[:, pr, :]).then_inc(S("o_stored"), 16)

            def group(g, gp):
                for s in range(GROUP_SLABS):
                    if s == 0 and gp is not None:
                        sp.wait_ge(S("a_done"), 2 * g)
                        load_lora(g)
                        sp.wait_ge(S("y_turned_ready"), 4 * g)
                        load_params(g)
                    load_slab(sp, slab_of(g, s) + 2, d["w_mix"][slab_of(g, s) + 2])
                    if gp is not None:
                        if s == 1:
                            store_rwkv(gp)
                        if s == 6:
                            store_fox(gp)
                    if s == 6:
                        sp.dma_start(g2_t[:], d["g2"][g]).then_inc(S("g2_landed"), 16)
                        sp.wait_ge(S("c_stored"), 32)
                        sp.wait_ge(S("aug_ones_ready"), 2)
                        cg = bass.ds(GH * g, GH) if gp is not None else slice(0, GH)
                        sp.dma_start(q_aug[HD + 1:HD + 2, :, :], c_dram[0:1, cg, :]).then_inc(S("c_rows_landed"), 16)
                        sp.dma_start(k_aug[HD:HD + 1, :, :], c_dram[1:2, cg, :]).then_inc(S("c_rows_landed"), 16)

            group_loop(sp, group)
            sp.wait_ge(weights_used, 2 * N_OUT)
            sp.wait_ge(S("y_rwkv_stored"), 32 * (GROUPS - 1))
            sp.wait_ge(S("o_stored"), 32 * (GROUPS - 1) + 1)
            for i in range(4):
                kt = TAIL_TILES[3 * i]
                sp.dma_start(in_lo[:, kt:kt + 3, :].bitcast(F32), y_dram[kt:kt + 3].rearrange("k p t -> p k t")
                             ).then_inc(S(f"y_landed_{i}"), 16)
            load_slab(sp, N_OUT + 2, d["w_mix"][N_OUT + 2])
            sp.wait_ge(S("in_ready"), 2 * KT)
            for i in range(4):
                sp.dma_start(h_t[:, 4 * i:4 * i + 4, :], x_quarter(i)).then_inc(S(f"input_landed_{i}"), 16)
            with sp.Fori(1, OUT_SLABS - 2) as o:
                load_slab(sp, N_OUT + 2 + o, d["w_mix"][N_OUT + 2 + o])
            with sp.Fori(0, 2) as i:
                load_slab(sp, N_FFN + i, d["w_gu"][i])
            sp.wait_ge(weights_used, 2 * N_FFN)
            sp.dma_start(p_raw[:], d["pT"]).then_inc(S("p_landed"), 16)
            with sp.Fori(2, 2 * CF) as i:
                load_slab(sp, N_FFN + i, d["w_gu"][i])
            with sp.Fori(0, OUT_SLABS) as o:
                load_slab(sp, down_base(0) + o, d["w_down"][o], down_cols)
            with sp.Fori(1, CHUNKS) as c:
                with sp.Fori(0, 2 * CF) as i:
                    load_slab(sp, ffn_base(c) + i, d["w_gu"][2 * CF * c + i])
                with sp.Fori(0, OUT_SLABS) as o:
                    load_slab(sp, down_base(c) + o, d["w_down"][OUT_SLABS * c + o], down_cols)
            for u in range(PROJ_SLABS):
                load_slab(sp, N_PROJ + u, d["ple_proj"][u])
            with sp.Fori(0, OUT_SLABS) as o:
                load_slab(sp, N_GATE + o, d["ple_gate"][o])

        @block.tensor
        def _(pe):
            for n in range(LORA_SLABS):
                multiply_slab(pe, n, n % 2, in_hi, in_lo,
                              input_ready=(lambda kt: pe.wait_ge(S("in_ready"), kt + 1)) if n == 0 else None)
                if n == 1:
                    pe.wait_ge(S("consts_landed"), 32)
                    pe.wait_ge(S("ones_landed"), 32)
                    pe.wait_ge(S("x_summed_dve"), KT // 2)
                    pe.wait_ge(S("x_summed_pool"), KT // 2)
                    for i in range(2):
                        last = nc.tensor.matmul(aux[:], ones[:], acc_x[:, i, :], start=i == 0, stop=i == 1,
                                                skip_group_check=True)
                    last.then_inc(S("norm_summed"), 1)

            def group(g, gp):
                for s in range(GROUP_SLABS):
                    def side(kt):
                        if s < 6:
                            if gp is not None:
                                pe_attention(pe, s, kt, gp)
                                pe_finish(pe, s, kt, gp)
                            pe_rwkv_prep(pe, s, kt, g)
                        else:
                            pe_fox_prep(pe, s, kt, g)
                            pe_recurrence(pe, s, kt, g)
                    multiply_slab(pe, slab_of(g, s), s % 2, in_hi, in_lo, side=side)

            group_loop(pe, group)

            def tail(st, s, kt):
                pe_attention(pe, s, kt, GROUPS - 1)
                pe_finish(pe, s, kt, GROUPS - 1)
                if st in multiplied_at:
                    i = multiplied_at[st]
                    if i == 0:
                        pe.wait_ge(tile_evacuated, N_OUT)
                        pe.wait_ge(lo_ready, 2 * N_OUT + 4)
                    pe.wait_ge(S("in_ready"), KT + i + 1)
                    k = TAIL_TILES[i]
                    for j in range(2):
                        three_products(psum[j][:], ring_slots(j, k // HALF), k % HALF * P, in_hi[:, k, :],
                                       in_lo[:, k, :], i == 0, False)
            tail_steps(tail)
            pe.wait_ge(S("in_ready"), 2 * KT)
            for j in range(2):
                s, k = ring_slots(j, 1), KT - 1
                w_h, w_l = (w[:, s, k % HALF * P:(k % HALF + 1) * P] for w in (w_hi, w_lo))
                nc.tensor.matmul(psum[j][:], w_h, in_hi[:, k, :], start=False, stop=False, skip_group_check=True)
                nc.tensor.matmul(psum[j][:], w_h, in_lo[:, k, :], start=False, stop=False, skip_group_check=True
                                 ).then_inc(weights_used, 1)
                nc.tensor.matmul(psum[j][:], w_l, in_hi[:, k, :], start=False, stop=True, skip_group_check=True
                                 ).then_inc(weights_used, 1)
            with pe.Fori(1, OUT_SLABS // 2) as i:
                for j in range(2):
                    multiply_slab(pe, N_OUT + 2 * i + j, j, in_hi, in_lo)

            def gate_up_pair(c, i, first):
                for j in range(2):
                    def side(kt):
                        if first and j == 0:
                            pe.wait_ge(S("hn_ready"), kt + 1)
                        if first and j == 0 and kt == 15:
                            pe.wait_ge(S("h_summed"), KT + 1)
                            nc.tensor.matmul(aux[:], ones[:], acc_h[:], start=True, stop=True,
                                             skip_group_check=True).then_inc(S("norm_summed"), 1)
                    multiply_slab(pe, ffn_base(c) + 2 * i + j, j, hn_hi, hn_lo, side=side)

            def down(c):
                with pe.Fori(0, OUT_SLABS // 2) as i:
                    for j in range(2):
                        def side(kt):
                            if j == 0 and kt == 0:
                                pe.wait_ge(S("low_part_ready"), 2 + CF * c + DOWN_HALVES[0])
                            if j == 0 and kt == DOWN_HALVES[0]:
                                pe.wait_ge(S("low_part_ready"), 2 + CF * c + CF)
                        multiply_slab(pe, down_base(c) + 2 * i + j, j, act_hi, act_lo, kts=DOWN_HALVES, side=side)

            gate_up_pair(0, 0, True)
            with pe.Fori(1, CF) as i:
                gate_up_pair(0, i, False)
            down(0)
            with pe.Fori(1, CHUNKS) as c:
                with pe.Fori(0, CF) as i:
                    gate_up_pair(c, i, False)
                down(c)
            pe.wait_ge(S("low_part_ready"), 2)
            for u in range(PROJ_SLABS):
                for r in range(PROJ_TILES):
                    tile = N_PROJ + PROJ_TILES * u + r
                    pe.wait_ge(tile_evacuated, tile - 1)
                    if r % 4 == 0:
                        pe.wait_ge(lo_ready, 2 * (N_PROJ + u) + r // 4 + 1)
                    for k in range(2):
                        last = three_products(psum[tile % 2][:], ring_slots(u % 2, r // 4), ((r % 4) * 2 + k) * P,
                                              p_hi[:, k, :], p_lo[:, k, :], k == 0, k == 1)
                    last.then_inc(weights_used if r % 4 == 3 else S("proj_done"), 1)
                if u == 0:
                    pe.wait_ge(S("h_summed"), 2 * KT + 2)
                    pe.wait_ge(S("norm_ready"), NORM_FFN)
                    nc.tensor.matmul(aux[:], ones[:], acc_h[:], start=True, stop=True).then_inc(S("norm_summed"), 1)

            def gate_slab(o, j, first):
                def side(kt):
                    if first and kt == 15:
                        pe.wait_ge(S("e_summed"), KT)
                        pe.wait_ge(S("norm_ready"), NORM_GATE)
                        nc.tensor.matmul(aux[:], ones[:], acc_e[:], start=True, stop=True,
                                         skip_group_check=True).then_inc(S("norm_summed"), 1)
                after(pe, tile_evacuated, TILE_GATE + o - 1)
                multiply_slab(pe, N_GATE + o, j, hn_hi, hn_lo, side=side)

            pe.wait_ge(S("hn_ready"), 2 * KT)
            gate_slab(0, 0, True)
            gate_slab(1, 1, False)
            with pe.Fori(1, OUT_SLABS // 2) as i:
                for j in range(2):
                    gate_slab(2 * i + j, j, False)

        @block.scalar
        def _(act):
            act.wait_ge(S("par_landed"), 16)
            nc.scalar.activation(scratch[mybir.EngineType.Activation][:, 0:2], par[:, 0:2], ACT.Copy)
            for kt in range(KT):
                if kt % 4 == 0 and kt < 8:
                    round_slab(act, 0, 0, halves=(kt // 4,))
                act.wait_ge(S(f"input_landed_{kt // 4}"), 16)
                nc.scalar.activation(in_hi[:, kt, :], x_raw[:, kt, :], ACT.Copy, scale=gain_of("attn_g")[:, kt:kt + 1]
                                     ).then_inc(S("in_hi_ready"), 1)
            round_slab(act, 1, 1)
            for kt in range(KT):
                if kt >= 4:
                    act.wait_ge(S("x_summed_dve" if kt % 2 == 0 else "x_summed_pool"), kt // 2 - 1)
                nc.scalar.activation(sqx[:, kt % 4, :], x_raw[:, kt, :], ACT.Square
                                     ).then_inc(S("x_squared_even" if kt % 2 == 0 else "x_squared_odd"), 1)

            def rstd(dst, norm):
                act.wait_ge(S("norm_summed"), norm)
                nc.scalar.activation(dst[:], aux[:], ACT.Ln, scale=1.0 / D_MODEL, bias=cb(CB_RMS)
                                     ).then_inc(S("norm_logged"), 1)
                act.wait_ge(S("norm_logged"), norm)
                nc.scalar.activation(dst[:], dst[:], ACT.Exp, scale=-0.5).then_inc(S("norm_ready"), 1)

            act.wait_ge(S("ones_landed"), 32)
            for n in range(1, LORA_SLABS):
                round_slab(act, n + 1, (n + 1) % 2)
                if n == 1:
                    rstd(rstd_x, NORM_X)
                act_arrival_lora(act, n - 1)

            def group(g, gp):
                for s in range(GROUP_SLABS):
                    if s == 0 and gp is None:
                        act_arrival_lora(act, LORA_SLABS - 1)
                    for kt in range(KT):
                        if s < 6:
                            if gp is not None:
                                act_attention(act, s, kt, gp)
                                act_finish(act, s, kt, gp)
                            act_rwkv_prep(act, s, kt, g)
                        else:
                            act_fox_prep(act, s, kt, g)
                            act_recurrence(act, s, kt, g)
                        if kt in ROUND_AT[s < 6]:
                            round_slab(act, slab_of(g, s) + 1, (s + 1) % 2, halves=(ROUND_AT[s < 6].index(kt),))

            group_loop(act, group)

            def tail(st, s, kt):
                act_attention(act, s, kt, GROUPS - 1)
                act_finish(act, s, kt, GROUPS - 1)
                if st in (1, 3):
                    round_slab(act, N_OUT + 1, 1, halves=(st // 2,))
                if st in cut_at:
                    i = cut_at[st]
                    k = TAIL_TILES[i]
                    if i < 12:
                        act.wait_ge(S(f"y_landed_{i // 3}"), 16)
                    elif k < HALF:
                        act.wait_ge(S("y_rwkv_ready"), 2 * GROUPS)
                    else:
                        act.wait_ge(S("o_ready"), 2 * (GROUPS - 1) + k - fox_tiles + 1)
                    if i == 0:
                        act.wait_ge(weights_used, 2 * N_OUT)
                    nc.scalar.activation(in_hi[:, k, :], tail_source(k), ACT.Copy).then_inc(S("in_hi_ready"), 1)
            tail_steps(tail)

            def out_pair(i, last):
                for j in range(2):
                    n = N_OUT + 2 * i + j
                    round_slab(act, n + 2, j)
                    ffn_norm[0](act, 2 * i + j, n, 2 * i + j, 1)
            pairs(act, OUT_SLABS // 2, out_pair)
            rstd(rstd_h, NORM_FFN)

            def gate_up_pair(c, i, last):
                for j in range(2):
                    n = ffn_base(c) + 2 * i + j
                    round_slab(act, n + 2, j, down_cols if last else gate_slab_cols)
                    t = CF * c + i
                    if j == 0:
                        act.wait_ge(tile_evacuated, n + 1)
                        nc.scalar.activation(silu_s[:], gate_s[:], ACT.Silu).then_inc(S("silu_ready"), 1)
                    else:
                        act.wait_ge(S("act_product_ready"), t + 1)
                        nc.scalar.activation(act_hi[:, i, :], up_s[:], ACT.Copy).then_inc(S("act_hi_ready"), 1)

            def down_pair(c, i, last, final):
                for j in range(2):
                    n = down_base(c) + 2 * i + j
                    round_slab(act, n + 2, j, gate_slab_cols if last else down_cols)
                    if final:
                        gate_norm[0](act, 2 * i + j, n, KT + 2 * i + j, 2)

            act.wait_ge(S("p_landed"), 16)
            for k in range(2):
                nc.scalar.activation(p_hi[:, k, :], p_raw[:, k, :], ACT.Copy).then_inc(S("p_hi_ready"), 1)
            with act.Fori(0, CHUNKS - 1) as c:
                pairs(act, CF, lambda i, last: gate_up_pair(c, i, last))
                pairs(act, OUT_SLABS // 2, lambda i, last: down_pair(c, i, last, False))
            pairs(act, CF, lambda i, last: gate_up_pair(CHUNKS - 1, i, last))
            pairs(act, OUT_SLABS // 2, lambda i, last: down_pair(CHUNKS - 1, i, last, True))
            for u in range(PROJ_SLABS):
                for r in range(PROJ_TILES):
                    t = PROJ_TILES * u + r
                    act.wait_ge(tile_evacuated, N_PROJ + t + 1)
                    after(act, S("e_summed"), t - 1)
                    nc.scalar.activation(sq_e[:, t % 2, :], e_t[:, t, :], ACT.Square).then_inc(S("e_squared"), 1)
                round_slab(act, N_GATE + u, u)
                if u == 0:
                    rstd(rstd_h, NORM_GATE)

            def gate_slot(o, j, last):
                if not last:
                    round_slab(act, N_GATE + o + 2, j)
                if isinstance(o, int) and o == 0:
                    rstd(rstd_e, NORM_E)
                act.wait_ge(tile_evacuated, TILE_GATE + o + 1)
                nc.scalar.activation(silu_s[:], gate_s[:], ACT.Sigmoid, bias=gain_of("gate_b")[:, o_col(o)]
                                     ).then_inc(S("gate_ready"), 1)

            gate_slot(0, 0, False)
            gate_slot(1, 1, False)
            with act.Fori(1, OUT_SLABS // 2 - 1) as i:
                for j in range(2):
                    gate_slot(2 * i + j, j, False)
            gate_slot(OUT_SLABS - 2, 0, True)
            gate_slot(OUT_SLABS - 1, 1, True)

        @block.vector
        def _(dve):
            dve.wait_ge(S("par_landed"), 16)
            for kt in range(KT):
                if kt % 4 == 0 and kt < 8:
                    subtract_slab(dve, 0, 0, halves=(kt // 4,))
                dve.wait_ge(S("in_hi_ready"), kt + 1)
                nc.vector.scalar_tensor_tensor(out=in_lo[:, kt, :], in0=x_raw[:, kt, :],
                                               scalar=gain_of("attn_g")[:, kt:kt + 1],
                                               in1=in_hi[:, kt, :].bitcast(F32), op0=ALU.mult, op1=ALU.subtract
                                               ).then_inc(S("in_ready"), 1)
            subtract_slab(dve, 1, 1)
            nc.vector.memset(scratch[mybir.EngineType.DVE][:, 0:1], 0.0).then_inc(S("o_stored"), 1)
            nc.vector.memset(acc_x[:, 0, :], 0.0).then_inc(S("acc_cleared"), 1)
            dve.wait_ge(S("acc_cleared"), 1)
            for i in range(KT // 2):
                dve.wait_ge(S("x_squared_even"), i + 1)
                after(dve, S("x_summed_dve"), i)
                nc.vector.tensor_tensor(acc_x[:, 0, :], acc_x[:, 0, :], sqx[:, 2 * (i % 2), :], ALU.add
                                        ).then_inc(S("x_summed_dve"), 1)
            nc.vector.tensor_scalar(qg8[:], gain_of("q_g"), HD ** -0.5, None, ALU.mult).then_inc(S("q_gain_ready"), 1)
            dve.wait_ge(S("ones_landed"), 32)
            dve.wait_ge(S("consts_landed"), 32)
            dve.wait_ge(S("q_gain_ready"), 1)
            dve.wait_ge(S("aug_ones_ready"), 2)
            dve.wait_ge(S("u_column_cleared"), 1)
            for n in range(1, LORA_SLABS):
                subtract_slab(dve, n + 1, (n + 1) % 2)
                dve_arrival_lora(dve, n - 1)

            def cut_next_slab(s, kt, g):
                if kt in SUBTRACT_AT[s < 6]:
                    subtract_slab(dve, slab_of(g, s) + 1, (s + 1) % 2, halves=(SUBTRACT_AT[s < 6].index(kt),))

            def group(g, gp):
                for s in range(GROUP_SLABS):
                    if s == 0:
                        if gp is None:
                            dve_arrival_lora(dve, LORA_SLABS - 1)
                        else:
                            dve_arrival_fox(dve, GROUP_SLABS, gp)
                    elif s <= 6:
                        dve_arrival_rwkv(dve, s, g)
                    else:
                        dve_arrival_fox(dve, s, g)
                    for kt in range(KT):
                        if s < 6:
                            if gp is not None:
                                dve_attention(dve, s, kt, gp)
                                dve_finish(dve, s, kt, gp)
                            dve_rwkv_prep(dve, s, kt, g)
                            cut_next_slab(s, kt, g)
                        else:
                            cut_next_slab(s, kt, g)
                            dve_fox_prep(dve, s, kt, g)
                            dve_recurrence(dve, s, kt, g)

            group_loop(dve, group)
            dve_arrival_fox(dve, GROUP_SLABS, GROUPS - 1)

            def tail(st, s, kt):
                dve_attention(dve, s, kt, GROUPS - 1)
                dve_finish(dve, s, kt, GROUPS - 1)
                if st in (2, 4):
                    subtract_slab(dve, N_OUT + 1, 1, halves=(st // 2 - 1,))
                if st in cut_at:
                    i = cut_at[st]
                    k = TAIL_TILES[i]
                    dve.wait_ge(S("in_hi_ready"), KT + i + 1)
                    nc.vector.tensor_tensor(in_lo[:, k, :], tail_source(k), in_hi[:, k, :].bitcast(F32), ALU.subtract
                                            ).then_inc(S("in_ready"), 1)
            tail_steps(tail)

            def add_to_residual(o, n, j):
                dve.wait_ge(weights_used, 2 * n + 2)
                nc.vector.tensor_tensor(h_t[:, o, :], h_t[:, o, :], psum[j][:], ALU.add).then_inc(tile_evacuated, 1)

            def out_pair(i, last):
                for j in range(2):
                    o, n = 2 * i + j, N_OUT + 2 * i + j
                    subtract_slab(dve, n + 2, j, halves=(0,))
                    add_to_residual(o, n, j)
                    subtract_slab(dve, n + 2, j, halves=(1,))
                    ffn_norm[1](dve, o, o)
            dve.wait_ge(S("input_landed_0"), 32)
            out_pair(0, False)
            for i in range(1, 4):
                dve.wait_ge(S(f"input_landed_{i}"), 32)
            with dve.Fori(1, OUT_SLABS // 2 - 1) as i:
                out_pair(i, False)
            out_pair(OUT_SLABS // 2 - 1, True)
            dve.wait_ge(S("norm_ready"), NORM_FFN)

            def gate_up_pair(c, i, last):
                for j in range(2):
                    n = ffn_base(c) + 2 * i + j
                    subtract_slab(dve, n + 2, j, down_cols if last else gate_slab_cols)
                    t = CF * c + i
                    dve.wait_ge(weights_used, 2 * n + 2)
                    if j == 0:
                        nc.vector.tensor_tensor(gate_s[:], psum[0][:], rstd_h[:], ALU.mult
                                                ).then_inc(tile_evacuated, 1)
                    else:
                        dve.wait_ge(S("low_part_ready"), 2 + t)
                        nc.vector.tensor_tensor(up_s[:], psum[1][:], rstd_h[:], ALU.mult
                                                ).then_inc(tile_evacuated, 1)
                        dve.wait_ge(tile_evacuated, n + 1)
                        dve.wait_ge(S("silu_ready"), t + 1)
                        nc.vector.tensor_tensor(up_s[:], up_s[:], silu_s[:], ALU.mult
                                                ).then_inc(S("act_product_ready"), 1)
                        dve.wait_ge(S("act_hi_ready"), t + 1)
                        nc.vector.tensor_tensor(act_lo[:, i, :], up_s[:], act_hi[:, i, :].bitcast(F32), ALU.subtract
                                                ).then_inc(S("low_part_ready"), 1)

            def down_pair(c, i, last, final):
                for j in range(2):
                    o, n = 2 * i + j, down_base(c) + 2 * i + j
                    next_cols = gate_slab_cols if last else down_cols
                    subtract_slab(dve, n + 2, j, next_cols, halves=(0,))
                    add_to_residual(o, n, j)
                    subtract_slab(dve, n + 2, j, next_cols, halves=(1,))
                    if final:
                        gate_norm[1](dve, o, KT + o)

            for k in range(2):
                dve.wait_ge(S("p_hi_ready"), k + 1)
                nc.vector.tensor_tensor(p_lo[:, k, :], p_raw[:, k, :], p_hi[:, k, :].bitcast(F32), ALU.subtract
                                        ).then_inc(S("low_part_ready"), 1)
            with dve.Fori(0, CHUNKS - 1) as c:
                pairs(dve, CF, lambda i, last: gate_up_pair(c, i, last))
                pairs(dve, OUT_SLABS // 2, lambda i, last: down_pair(c, i, last, False))
            pairs(dve, CF, lambda i, last: gate_up_pair(CHUNKS - 1, i, last))
            pairs(dve, OUT_SLABS // 2, lambda i, last: down_pair(CHUNKS - 1, i, last, True))
            for u in range(PROJ_SLABS):
                for r in range(PROJ_TILES):
                    t = PROJ_TILES * u + r
                    if r % 4 == 3:
                        dve.wait_ge(weights_used, 2 * (N_PROJ + u) + r // 4 + 1)
                    else:
                        dve.wait_ge(S("proj_done"), 3 * (t // 4) + t % 4 + 1)
                    nc.vector.tensor_copy(e_t[:, t, :], psum[(N_PROJ + t) % 2][:]).then_inc(tile_evacuated, 1)
                subtract_slab(dve, N_GATE + u, u)

            def gate_slot(o, j, last):
                n = N_GATE + o
                if not last:
                    subtract_slab(dve, n + 2, j)
                if isinstance(o, int) and o == 0:
                    dve.wait_ge(S("norm_ready"), NORM_GATE)
                    dve.wait_ge(S("norm_ready"), NORM_E)
                if not (isinstance(o, int) and o == 0):
                    dve.wait_ge(S("out_ready"), o)
                nc.vector.scalar_tensor_tensor(out=up_s[:], in0=e_t[:, o, :], scalar=gain_of("ple_g")[:, o_col(o)],
                                               in1=rstd_e[:], op0=ALU.mult, op1=ALU.mult).then_inc(S("e_ready"), 1)
                dve.wait_ge(weights_used, 2 * n + 2)
                nc.vector.tensor_tensor(gate_s[:], psum[j][:], rstd_h[:], ALU.mult
                                        ).then_inc(tile_evacuated, 1)
                dve.wait_ge(S("gate_ready"), o + 1)
                dve.wait_ge(S("e_ready"), o + 1)
                nc.vector.tensor_tensor(up_s[:], up_s[:], silu_s[:], ALU.mult).then_inc(S("gated"), 1)
                dve.wait_ge(S("gated"), o + 1)
                nc.vector.tensor_tensor(h_t[:, o, :], h_t[:, o, :], up_s[:], ALU.add).then_inc(S("out_ready"), 1)

            gate_slot(0, 0, False)
            gate_slot(1, 1, False)
            with dve.Fori(1, OUT_SLABS // 2 - 1) as i:
                for j in range(2):
                    gate_slot(2 * i + j, j, False)
            gate_slot(OUT_SLABS - 2, 0, True)
            gate_slot(OUT_SLABS - 1, 1, True)

        @block.gpsimd
        def _(pool):
            nc.gpsimd.memset(scratch[mybir.EngineType.Pool][:], 0.0)
            nc.gpsimd.memset(acc_x[:, 1, :], 0.0).then_inc(S("sums_cleared"), 1)
            pool.wait_ge(S("sums_cleared"), 1)
            for i in range(KT // 2):
                pool.wait_ge(S("x_squared_odd"), i + 1)
                after(pool, S("x_summed_pool"), i)
                nc.gpsimd.tensor_tensor(acc_x[:, 1, :], acc_x[:, 1, :], sqx[:, 2 * (i % 2) + 1, :], ALU.add
                                        ).then_inc(S("x_summed_pool"), 1)
            pool.wait_ge(S("in_ready"), KT)
            pool.wait_ge(S("x_summed_dve"), KT // 2)
            pool.wait_ge(S("x_summed_pool"), KT // 2)
            nc.gpsimd.memset(u_t[:, 0:1], 0.0).then_inc(S("u_column_cleared"), 1)
            pool.wait_ge(S("u_column_cleared"), 1)
            for i, t in enumerate((q_aug, k_aug)):
                after(pool, S("aug_ones_ready"), i)
                nc.gpsimd.memset(t[HD:HD + 2, :, :], 1.0).then_inc(S("aug_ones_ready"), 1)
            pool.wait_ge(S("aug_ones_ready"), 2)
            pool.wait_ge(S("consts_landed"), 32)
            for n in range(1, LORA_SLABS):
                pool_arrival_lora(pool, n - 1)

            def group(g, gp):
                for s in range(GROUP_SLABS):
                    if s == 0:
                        if gp is None:
                            pool_arrival_lora(pool, LORA_SLABS - 1)
                    for kt in range(KT):
                        if s < 6:
                            if gp is not None:
                                pool_attention(pool, s, kt, gp)
                                pool_finish(pool, s, kt, gp)
                            pool_rwkv_prep(pool, s, kt, g)
                        else:
                            pool_recurrence(pool, s, kt, g)

            group_loop(pool, group)
            for s in range(6):
                for kt in range(KT):
                    pool_attention(pool, s, kt, GROUPS - 1)
                    pool_finish(pool, s, kt, GROUPS - 1)
            pool.wait_ge(S("in_ready"), 2 * KT)
            nc.gpsimd.memset(acc_h[:], 0.0).then_inc(S("h_summed"), 1)

            def sum_squares(first):
                with pool.Fori(0, KT) as o:
                    ffn_norm[2](pool, first + o)
            sum_squares(0)
            pool.wait_ge(S("norm_summed"), NORM_FFN)
            nc.gpsimd.memset(acc_h[:], 0.0).then_inc(S("h_summed"), 1)
            sum_squares(KT)
            pool.wait_ge(weights_used, 2 * N_PROJ)
            nc.gpsimd.memset(acc_e[:], 0.0).then_inc(S("sums_cleared"), 1)
            pool.wait_ge(S("sums_cleared"), 2)
            for o in range(KT):
                pool.wait_ge(S("e_squared"), o + 1)
                after(pool, S("e_summed"), o)
                nc.gpsimd.tensor_tensor(acc_e[:], acc_e[:], sq_e[:, o % 2, :], ALU.add).then_inc(S("e_summed"), 1)
            with pool.Fori(0, OUT_SLABS) as o:
                pool.wait_ge(S("out_ready"), o + 1)
                pool.dma_start(d["out"][o], h_t[:, o, :]).then_inc(S("out_stored"), 16)
            pool.wait_ge(S("out_stored"), 16 * OUT_SLABS)


def tiles(w):
    k, n = w.shape
    return w.reshape(k // P, P, n // P, P).transpose(2, 1, 0, 3).reshape(n // P, P, k)


def columns(v):
    return v.reshape(-1, P).T


def kernel(x, p, attn_norm_g, w_in, shift_mu, w0, w2, a0, a2, g2, k_k, k_a, r_k, lnx_g, lnx_b, q_norm_g,
           k_norm_g, fgate_b, w_out, ffn_norm_g, w_gate, w_up, w_down, ple_proj, ple_norm_g, ple_gate_norm_g,
           ple_gate_w, ple_gate_b):
    import numpy as np
    import concourse.bacc as bacc
    from concourse.bass_utils import run_bass_kernel_spmd

    A = lambda v: np.asarray(v)[0]
    wi, mu = A(w_in), A(shift_mu)
    RW = 1024
    lora0 = 3 * RW
    fox0 = lora0 + 2 * LORA + 2 * P
    f0 = fox0 + 3 * RW
    z = lambda *s: np.zeros(s, np.float32)
    parts = [wi[:, lora0:lora0 + LORA], wi[:, f0:f0 + 16], z(D_MODEL, P - LORA - 16),
             wi[:, lora0 + LORA:lora0 + 2 * LORA], z(D_MODEL, P - LORA), wi[:, lora0 + 2 * LORA:fox0]]
    for g in range(GROUPS):
        for ft in range(2):
            c = P * (2 * g + ft)
            parts += [wi[:, RW + c:RW + c + P], wi[:, c:c + P], wi[:, 2 * RW + c:2 * RW + c + P]]
        for kind in range(3):
            c = fox0 + RW * kind + 2 * P * g
            parts.append(wi[:, c:c + 2 * P])
    w_mix = np.concatenate([tiles(np.concatenate(parts, 1)), tiles(A(w_out))])
    gu = np.stack([tiles(A(w_gate)), tiles(A(w_up))], 1).reshape(2 * D_FF // P, P, D_MODEL)
    down = np.concatenate([tiles(A(w_down)[c * CF * P:(c + 1) * CF * P]) for c in range(CHUNKS)])
    proj = tiles(A(ple_proj)).reshape(PROJ_SLABS, PROJ_TILES, P, 2 * P).transpose(0, 2, 1, 3).reshape(
        PROJ_SLABS, P, D_MODEL)

    par = z(P, N_PAR)
    put = lambda name, v: par.__setitem__((slice(None), slice(PAR[name][0], PAR[name][0] + v.shape[1])), v)
    for name, v in (("attn_g", attn_norm_g), ("ffn_g", ffn_norm_g), ("gate_g", ple_gate_norm_g),
                    ("ple_g", ple_norm_g), ("gate_b", ple_gate_b)):
        put(name, columns(A(v)))
    lora_mu = z(P, 4)
    lora_mu[:LORA, 0] = mu[lora0:lora0 + LORA]
    lora_mu[:LORA, 1] = mu[lora0 + LORA:lora0 + 2 * LORA]
    lora_mu[:, 2:] = columns(mu[lora0 + 2 * LORA:])
    put("mu", lora_mu)
    par[LORA:LORA + 16, PAR["f_bias"][0]] = A(fgate_b)
    put("q_g", np.concatenate([A(q_norm_g)] * 2)[:, None])
    put("k_g", np.concatenate([A(k_norm_g)] * 2)[:, None])
    per_feature = [mu[RW:2 * RW], mu[:RW], mu[2 * RW:3 * RW], A(k_k), A(k_a), A(r_k).reshape(RW), A(w0), A(a0),
                   A(lnx_g), A(lnx_b)]
    g_params = np.stack([v.reshape(GROUPS, 2, P) for v in per_feature], -1).transpose(0, 2, 1, 3)

    i, j = np.arange(P)[:, None], np.arange(P)[None, :]
    mats = [i == j, np.ones((P, P)), i // HD == j // HD, i < j, i <= j]
    mats += [(i >> (m + 1) == j >> (m + 1)) & ((i >> m) & 1 == 0) & ((j >> m) & 1 == 1) for m in range(LEVELS + 1)]
    col = z(P, 8)
    col[:, :3] = [RMS_EPS, GN_EPS, 8 * math.log(2.0)]
    consts = np.concatenate([m.astype(np.float32) for m in mats] + [col], 1)
    import ml_dtypes
    id16 = np.concatenate([(i == j).astype(np.float32), np.where(j > i, np.float32(-1e30), np.float32(0))], 1
                          ).astype(ml_dtypes.bfloat16)

    arrays = {
        "xT": A(x).T.reshape(KT, P, SEQ), "pT": A(p)[0].T.reshape(2, P, SEQ).transpose(1, 0, 2),
        "w_mix": w_mix, "w_gu": gu, "w_down": down, "ple_proj": proj, "ple_gate": tiles(A(ple_gate_w)),
        "w2": A(w2).reshape(LORA, GROUPS, 2 * P).transpose(1, 0, 2),
        "a2": A(a2).reshape(LORA, GROUPS, 2 * P).transpose(1, 0, 2),
        "g2": A(g2).reshape(2, P, GROUPS, 2 * P).transpose(2, 1, 0, 3),
        "params": par, "g_params": g_params, "consts": consts, "id16": id16,
    }
    arrays = {k: np.ascontiguousarray(v) for k, v in arrays.items()}
    nc = bacc.Bacc("TRN2", target_bir_lowering=False, num_devices=1)
    d = {k: nc.dram_tensor(k, v.shape, mybir.dt.from_np(v.dtype), kind="ExternalInput").ap()
         for k, v in arrays.items()}
    d["out"] = nc.dram_tensor("out", [KT, P, SEQ], F32, kind="ExternalOutput").ap()
    layer(nc, d)
    r = run_bass_kernel_spmd(nc, [arrays], core_ids=[0])
    return r.results[0]["out"].reshape(D_MODEL, SEQ).T[None].copy()
```
